# Optimizing a Trainium2 kernel written in Bass

```python
import jax, jax.numpy as jnp
from jax import lax
import numpy as np

D_MODEL = 1024
BATCH = 1
SEQ = 2048
DEPTH = 1

N_META = 16
CONV_WIDTH = 512
CONV_K = 31
N_HEADS = 8
HEAD_DIM = 64
ATTN_WIDTH = N_HEADS * HEAD_DIM
Q_BLOCK = 128
N_GROUPS = 8
EXPERTS_PER_GROUP = 8
N_EXPERTS = N_GROUPS * EXPERTS_PER_GROUP
TOP_K = 2
D_EXPERT = 256
ROW_BLOCK = 256
RMS_EPS = 1e-6
LN_EPS = 1e-5

IN_SPLITS = (2 * CONV_WIDTH, ATTN_WIDTH, ATTN_WIDTH, ATTN_WIDTH, N_HEADS, D_MODEL, D_MODEL)
IN_COLS = sum(IN_SPLITS)

kernel_name = "hybrid_conformer_fox_hmoe_block"

def rmsnorm(x, g):
    xf = x.astype(jnp.float32)
    y = xf * lax.rsqrt(jnp.mean(xf * xf, axis=-1, keepdims=True) + RMS_EPS)
    return (y * g.astype(jnp.float32)).astype(x.dtype)

def layernorm(x, g, b):
    xf = x.astype(jnp.float32)
    mu = jnp.mean(xf, axis=-1, keepdims=True)
    var = jnp.mean(jnp.square(xf - mu), axis=-1, keepdims=True)
    y = (xf - mu) * lax.rsqrt(var + LN_EPS)
    return (y * g.astype(jnp.float32) + b.astype(jnp.float32)).astype(x.dtype)

def conformer_conv(u, dw_w, dw_b, ln_g, ln_b, w_pw, b_pw):
    a = u[..., :CONV_WIDTH] * jax.nn.sigmoid(u[..., CONV_WIDTH:])
    a = lax.conv_general_dilated(a, dw_w[:, None, :], window_strides=(1,),
                                 padding=[(CONV_K - 1, 0)],
                                 dimension_numbers=('NWC', 'WIO', 'NWC'),
                                 feature_group_count=CONV_WIDTH) + dw_b
    a = jax.nn.silu(layernorm(a, ln_g, ln_b))
    return a @ w_pw + b_pw

def forgetting_attention(q, k, v, logf):
    L = q.shape[1]
    c = jnp.cumsum(logf, axis=1).transpose(0, 2, 1)
    scale = HEAD_DIM ** -0.5

    def block(q0, q1):
        t = jnp.arange(q0, q1)
        s = jnp.arange(q1)
        logits = jnp.einsum('bqhd,bkhd->bhqk', q[:, q0:q1], k[:, :q1]).astype(jnp.float32) * scale
        logits = logits + c[:, :, q0:q1, None] - c[:, :, None, :q1]
        logits = jnp.where(s[None, :] <= t[:, None], logits, -jnp.inf)
        p = jax.nn.softmax(logits, axis=-1)
        return jnp.einsum('bhqk,bkhd->bqhd', p.astype(v.dtype), v[:, :q1])

    n_blocks = (L - N_META) // Q_BLOCK
    bounds = [(0, N_META)] + [(N_META + i * Q_BLOCK, N_META + (i + 1) * Q_BLOCK) for i in range(n_blocks)]
    return jnp.concatenate([block(q0, q1) for (q0, q1) in bounds], axis=1)

def hierarchical_moe(xt, w_group, b_group, w_router, b_router, w_gate, w_up, w_down):
    N = xt.shape[0]
    g_logits = (xt @ w_group).astype(jnp.float32) + b_group.astype(jnp.float32)
    g_prob = jax.nn.softmax(g_logits, axis=-1)
    g_idx = jnp.argmax(g_logits, axis=-1).astype(jnp.int32)
    g_w = jnp.take_along_axis(g_prob, g_idx[:, None], axis=1)
    e_logits = ((xt @ w_router).astype(jnp.float32) + b_router.astype(jnp.float32)).reshape(N, N_GROUPS, EXPERTS_PER_GROUP)
    e_logits = jnp.take_along_axis(e_logits, g_idx[:, None, None], axis=1)[:, 0]
    top_l, top_i = lax.top_k(e_logits, TOP_K)
    w = jax.nn.softmax(top_l, axis=-1) * g_w

    A = N * TOP_K
    e_id = (g_idx[:, None] * EXPERTS_PER_GROUP + top_i.astype(jnp.int32)).reshape(A)
    tok = jnp.repeat(jnp.arange(N, dtype=jnp.int32), TOP_K)
    wa = w.reshape(A)

    order = jnp.argsort(e_id)
    se, stok, sw = e_id[order], tok[order], wa[order]
    counts = jnp.zeros((N_EXPERTS,), jnp.int32).at[e_id].add(1)
    start = jnp.cumsum(counts) - counts
    padded = (counts + ROW_BLOCK - 1) // ROW_BLOCK * ROW_BLOCK
    pend = jnp.cumsum(padded)
    pstart = pend - padded
    dest = pstart[se] + jnp.arange(A, dtype=jnp.int32) - start[se]

    n_blocks = -(-A // ROW_BLOCK) + N_EXPERTS
    P = n_blocks * ROW_BLOCK
    buf_tok = jnp.full((P,), N, jnp.int32).at[dest].set(stok)
    buf_w = jnp.zeros((P,), jnp.float32).at[dest].set(sw)
    blk_e = jnp.minimum(jnp.searchsorted(pend, jnp.arange(n_blocks, dtype=jnp.int32) * ROW_BLOCK, side='right'),
                        N_EXPERTS - 1).astype(jnp.int32)

    x_pad = jnp.concatenate([xt, jnp.zeros((1, xt.shape[1]), xt.dtype)], axis=0)
    xin = x_pad[buf_tok].reshape(n_blocks, ROW_BLOCK, xt.shape[1])

    def expert_block(args):
        xb, e = args
        hb = jax.nn.silu(xb @ w_gate[e]) * (xb @ w_up[e])
        return hb @ w_down[e]

    yb = lax.map(expert_block, (xin, blk_e)).reshape(P, xt.shape[1])
    y = yb.astype(jnp.float32) * buf_w[:, None]
    out = jax.ops.segment_sum(y, buf_tok, num_segments=N + 1)[:N]
    return out.astype(xt.dtype)

def setup_inputs(seed: int = 0) -> dict:
    key = jax.random.key(seed)
    ks = jax.random.split(key, 24)
    f32 = jnp.float32
    nrm = lambda k, shape, scale: jax.random.normal(k, shape, f32) * scale
    return {
        "x": nrm(ks[0], (BATCH, SEQ, D_MODEL), 1.0),
        "meta": nrm(ks[1], (N_META, D_MODEL), 1.0),
        "norm1_g": 1.0 + nrm(ks[2], (DEPTH, D_MODEL), 0.02),
        "w_in": nrm(ks[3], (DEPTH, D_MODEL, IN_COLS), D_MODEL ** -0.5),
        "b_in": nrm(ks[4], (DEPTH, IN_COLS), 0.02),
        "dw_w": nrm(ks[5], (DEPTH, CONV_K, CONV_WIDTH), CONV_K ** -0.5),
        "dw_b": nrm(ks[6], (DEPTH, CONV_WIDTH), 0.02),
        "conv_ln_g": 1.0 + nrm(ks[7], (DEPTH, CONV_WIDTH), 0.02),
        "conv_ln_b": nrm(ks[8], (DEPTH, CONV_WIDTH), 0.02),
        "w_conv_out": nrm(ks[9], (DEPTH, CONV_WIDTH, D_MODEL), CONV_WIDTH ** -0.5),
        "b_conv_out": nrm(ks[10], (DEPTH, D_MODEL), 0.02),
        "q_norm_g": 1.0 + nrm(ks[11], (DEPTH, HEAD_DIM), 0.02),
        "k_norm_g": 1.0 + nrm(ks[12], (DEPTH, HEAD_DIM), 0.02),
        "b_forget": jax.random.uniform(ks[13], (DEPTH, N_HEADS), f32, 1.0, 3.0),
        "w_attn_out": nrm(ks[14], (DEPTH, ATTN_WIDTH, D_MODEL), ATTN_WIDTH ** -0.5),
        "w_out": nrm(ks[15], (DEPTH, D_MODEL, D_MODEL), D_MODEL ** -0.5),
        "norm2_g": 1.0 + nrm(ks[16], (DEPTH, D_MODEL), 0.02),
        "w_group": nrm(ks[17], (DEPTH, D_MODEL, N_GROUPS), D_MODEL ** -0.5),
        "b_group": nrm(ks[18], (DEPTH, N_GROUPS), 0.01),
        "w_router": nrm(ks[19], (DEPTH, D_MODEL, N_EXPERTS), D_MODEL ** -0.5),
        "b_router": nrm(ks[20], (DEPTH, N_EXPERTS), 0.01),
        "w_gate": nrm(ks[21], (DEPTH, N_EXPERTS, D_MODEL, D_EXPERT), D_MODEL ** -0.5),
        "w_up": nrm(ks[22], (DEPTH, N_EXPERTS, D_MODEL, D_EXPERT), D_MODEL ** -0.5),
        "w_down": nrm(ks[23], (DEPTH, N_EXPERTS, D_EXPERT, D_MODEL), D_EXPERT ** -0.5),
    }

def reference(x, meta, norm1_g, w_in, b_in, dw_w, dw_b, conv_ln_g, conv_ln_b, w_conv_out, b_conv_out,
              q_norm_g, k_norm_g, b_forget, w_attn_out, w_out, norm2_g, w_group, b_group, w_router,
              b_router, w_gate, w_up, w_down):
    B = x.shape[0]
    h = jnp.concatenate([jnp.broadcast_to(meta[None].astype(x.dtype), (B, N_META, D_MODEL)), x], axis=1)
    L = h.shape[1]
    split_pts = list(np.cumsum(IN_SPLITS)[:-1])
    for l in range(DEPTH):
        xn = rmsnorm(h, norm1_g[l])
        proj = xn @ w_in[l] + b_in[l]
        u_conv, q, k, v, f_logit, gate_c, gate_a = jnp.split(proj, split_pts, axis=-1)

        y_conv = conformer_conv(u_conv, dw_w[l], dw_b[l], conv_ln_g[l], conv_ln_b[l],
                                w_conv_out[l], b_conv_out[l])

        q = rmsnorm(q.reshape(B, L, N_HEADS, HEAD_DIM), q_norm_g[l])
        k = rmsnorm(k.reshape(B, L, N_HEADS, HEAD_DIM), k_norm_g[l])
        v = v.reshape(B, L, N_HEADS, HEAD_DIM)
        logf = jax.nn.log_sigmoid(f_logit.astype(jnp.float32) + b_forget[l].astype(jnp.float32))
        o = forgetting_attention(q, k, v, logf).reshape(B, L, ATTN_WIDTH)
        y_attn = o @ w_attn_out[l]

        merged = jax.nn.sigmoid(gate_c) * y_conv + jax.nn.sigmoid(gate_a) * y_attn
        h = h + merged @ w_out[l]

        hn = rmsnorm(h, norm2_g[l]).reshape(B * L, D_MODEL)
        y_moe = hierarchical_moe(hn, w_group[l], b_group[l], w_router[l], b_router[l],
                                 w_gate[l], w_up[l], w_down[l])
        h = h + y_moe.reshape(B, L, D_MODEL)
    return h[:, N_META:]


_drawn_inputs = setup_inputs


def setup_inputs(seed=0):
    import zlib

    import numpy as np

    out = dict(_drawn_inputs(seed))
    spreads = {}
    factors = {'norm1_g': 3.673,
     'b_in': 2.807,
     'conv_ln_g': 3.786,
     'conv_ln_b': 4.315,
     'b_conv_out': 3.013,
     'q_norm_g': 6.257,
     'k_norm_g': 5.761,
     'norm2_g': 2.751,
     'b_group': 4.077,
     'b_router': 6.298}
    for name, (base, spread) in spreads.items():
        noise = np.random.default_rng([zlib.crc32(name.encode()), seed]).standard_normal(out[name].shape)
        drawn = base * np.exp(spread * noise) if base else spread * noise
        out[name] = __import__('jax').numpy.asarray(drawn.astype(out[name].dtype))
    for name, factor in factors.items():
        out[name] = (out[name] * factor).astype(out[name].dtype)
    return out
```

```python
from contextlib import ExitStack

import concourse.bass as bass
import concourse.mybir as mybir
from concourse.alu_op_type import AluOpType as ALU

F32 = mybir.dt.float32
F32R = mybir.dt.float32r
BF16 = mybir.dt.bfloat16
I32 = mybir.dt.int32
U32 = mybir.dt.uint32
ACT = mybir.ActivationFunctionType
AX = mybir.AxisListType

P = 128
D = 1024
DC = D // P
SEQ = 2048
META = 16
L = META + SEQ
NT = SEQ // P
CW = 512
CT = CW // P
TAPS = 31
HEADS = 8
HD = 64
PAIRS = HEADS // 2
GROUPS = 8
PER_GROUP = 8
EXPERTS = GROUPS * PER_GROUP
DE = 256
RMS_EPS = 1e-6
LN_EPS = 1e-5
PAD = P - META
KT = NT + 1
KCOLS = KT * P

COL_Q = 2 * CW
COL_K = COL_Q + HEADS * HD
COL_V = COL_K + HEADS * HD
COL_F = COL_V + HEADS * HD
COL_G = COL_F + HEADS
CHUNKS = [(0, 412), (412, 412), (824, 412), (1236, 414), (1650, 414)]
XCHUNKS = [(META + 512 * i, 512) for i in range(SEQ // 512)]
TAP_SLOTS = 32


def register_waits(sem):
    passed = {}

    def wait(eng, semaphore, value):
        eng.wait_ge(semaphore, value)
        if not isinstance(value, int):
            key = str(eng.engine).split(".")[-1]
            if key not in passed:
                passed[key] = sem(f"waits_passed_{key}")
            eng.sem_inc(passed[key], 1)

    return wait


def raw(ap):
    return ap.bitcast(F32)


def pair_matmuls(pe, out, lhs, rhs, first, last):
    pe.matmul(out, lhs[0], rhs[0], start=first, stop=False)
    pe.matmul(out, lhs[0], rhs[1], start=False, stop=False)
    return pe.matmul(out, lhs[1], rhs[0], start=False, stop=last)


def stage_project(nc, x, meta, norm1_g, w_in, b_in, dw_w, dw_b, q_norm_g, k_norm_g, b_forget,
                  conv_d, gate_d, qk_d, v_d, decay_d):
    with ExitStack() as ctx:
        def sb(name, shape, dt=F32):
            return ctx.enter_context(nc.sbuf_tensor("project_" + name, shape, dt))

        def sem(name):
            return nc.alloc_semaphore("project_" + name)

        wait = register_waits(sem)

        xnT_hi = sb("xnT_hi", [P, DC, L], F32R)
        xnT_lo = sb("xnT_lo", [P, DC, L], F32R)
        w_raw = sb("w_raw", [P, 2, DC, P])
        w_hi = sb("w_hi", [P, 2, DC, P], F32R)
        w_lo = sb("w_lo", [P, 2, DC, P], F32R)
        work = sb("work", [P, 5, KCOLS])
        ident = sb("ident", [P, P])
        head_ones = sb("head_ones", [P, P])
        bias = sb("bias", [P, 36])
        gain = sb("gain", [P, 8])
        gain_raw = sb("gain_raw", [P, 2])
        gain_bias = sb("gain_bias", [P, 8])
        taps = sb("taps", [P, CT, TAP_SLOTS])
        conv_bias = sb("conv_bias", [P, CT])
        f_bias = sb("f_bias", [HEADS, 3])
        eps = sb("eps", [P, 1])
        stat = sb("stat", [P, 2, 8])
        sq = sb("sq", [P, 2, 414])
        root = sb("root", [P, 2, 414])
        inv_root = sb("inv_root", [P, 2, 414])
        bank = ctx.enter_context(nc.psum_tensor("project_bank", [P, 8, 512], F32))

        consts_zero = sem("consts_zero")
        consts_ready = sem("consts_ready")
        taps_zeroed = sem("taps_zeroed")
        norm_gain_loaded = sem("norm_gain_loaded")
        param_loaded = sem("param_loaded")
        x_loaded = [sem("x_loaded0"), sem("x_loaded1")]
        squares_summed = sem("squares_summed")
        var_ready = sem("var_ready")
        root_ready = sem("root_ready")
        newton_step = sem("newton_step")
        xn_ready = sem("xn_ready")
        xn_turned = sem("xn_turned")
        xn_hi_ready = sem("xn_hi_ready")
        xn_lo_ready = sem("xn_lo_ready")
        w_loaded = [sem("w_loaded0"), sem("w_loaded1")]
        w_hi_ready = sem("w_hi_ready")
        w_split = sem("w_split")
        chunk_done = sem("chunk_done")
        tile_done = sem("tile_done")
        bank_read = [sem(f"bank_read{i}") for i in range(5)]
        setup_step = sem("setup_step")
        params_ready = sem("params_ready")
        gate_stored = [sem("gate_stored0"), sem("gate_stored1")]
        tap_done = sem("tap_done")
        conv_stored = sem("conv_stored")
        sum_ready = sem("sum_ready")
        root2_ready = sem("root2_ready")
        inv_ready = sem("inv_ready")
        qn_ready = sem("qn_ready")
        q_hi_ready = sem("q_hi_ready")
        q_lo_ready = sem("q_lo_ready")
        qk_stored = [sem("qk_stored0"), sem("qk_stored1")]
        v_pad_ready = sem("v_pad_ready")
        v_turned = sem("v_turned")
        v_hi_ready = sem("v_hi_ready")
        v_lo_ready = sem("v_lo_ready")
        v_stored = [sem("v_stored0"), sem("v_stored1")]
        f_vec = sem("f_vec")
        f_act = sem("f_act")
        decay_stored = sem("decay_stored")

        w_cols = w_in.rearrange("(c p) n -> p c n", p=P)
        x_tiles = x.rearrange("(t p) d -> t p d", p=P)

        LATER_FIRST = [CHUNKS[i] for i in (1, 2, 3, 0, 4)]
        FRONT_CHUNKS = [LATER_FIRST, LATER_FIRST, XCHUNKS, XCHUNKS, XCHUNKS, XCHUNKS]
        N_FRONT, N_QK, N_V = 6 * CT, 2 * PAIRS, PAIRS
        FRONT_COUNT = [sum(len(c) - 1 for c in FRONT_CHUNKS[:j]) for j in range(7)]
        QK_COUNT = CT * FRONT_COUNT[6]
        V_COUNT = QK_COUNT + 4 * N_QK
        F_COUNT = V_COUNT + 4 * N_V
        XN = [0, 1]
        XIN = [3, 4]

        def wait_chunk(eng, n, counted, i, chunks):
            if i < len(chunks) - 1:
                wait(eng, chunk_done, counted + (i + 1))
            else:
                wait(eng, tile_done, n + 3)

        def value_half(b, t, tiles, half):
            v = work[:, 1 + 2 * b:3 + 2 * b, :].rearrange("p s n -> p (s n)")
            return v.rearrange("p (t h k e) -> p t h k e", h=2, k=2, e=HD)[:, t:t + tiles, :, half, :]

        def over_pair_tiles(eng, tile):
            for b in range(2):
                tile(0, b)
            with eng.Fori(1, N_QK // 2 - 1) as it:
                for b in range(2):
                    tile(it, b)
            for b in range(2):
                tile(N_QK // 2 - 1, b)

        block = ctx.enter_context(nc.Block())

        @block.sync
        def _(sp):
            def load_w(n, b, col, width=P):
                wait(sp, w_split, n + 1)
                sp.dma_start(w_raw[:, b, :, 0:width], w_cols[:, :, bass.ds(col, width)])\
                  .then_inc(w_loaded[b], 16)

            def load_convolution(ct):
                load_w(ct * 6, 0, ct * P + CW)
                load_w(ct * 6 + 1, 1, ct * P)

            def load_tokens(it, b):
                wait(sp, xn_ready, it * 2 + (b + 1))
                sp.dma_start(work[:, XIN[b], 0:D], x_tiles[it * 2 + b]).then_inc(x_loaded[b], 16)

            load_tokens(0, 0)
            sp.dma_start(work[:, 2, 0:D], norm1_g.rearrange("(o d) -> o d", o=1).to_broadcast([P, D]))\
              .then_inc(norm_gain_loaded, 16)
            load_tokens(0, 1)
            with sp.Fori(1, 3) as it:
                for b in range(2):
                    load_tokens(it, b)
            load_convolution(0)
            with sp.Fori(3, NT // 2) as it:
                for b in range(2):
                    load_tokens(it, b)
            wait(sp, xn_ready, NT + 1)
            sp.dma_start(work[0:META, XIN[0], 0:D], meta).then_inc(x_loaded[0], 16)

            def load_gates(ct):
                for j in range(4):
                    load_w(ct * 6 + (2 + j), j % 2, ct * (4 * P) + (COL_G + j * P))

            with sp.Fori(0, CT - 1) as ct:
                load_gates(ct)
                load_convolution(ct + 1)
            load_gates(CT - 1)

            def store_pair(it, b):
                wait(sp, q_hi_ready, it * 10 + (5 * b + 5))
                wait(sp, q_lo_ready, it * 10 + (5 * b + 10))
                for half in range(2):
                    sp.dma_start(qk_d[it * 2 + b, half], work[:, 1 + 2 * b + half, 0:L])\
                      .then_inc(qk_stored[b], 16)

            with sp.Fori(0, 2) as it:
                for b in range(2):
                    load_w(it * 2 + (N_FRONT + b), b, it * (2 * P) + (COL_Q + b * P))
            with sp.Fori(2, N_QK // 2) as it:
                for b in range(2):
                    store_pair(it - 2, b)
                    load_w(it * 2 + (N_FRONT + b), b, it * (2 * P) + (COL_Q + b * P))
            with sp.Fori(0, N_V // 2) as it:
                for b in range(2):
                    store_pair(it + (N_QK // 2 - 2), b)
                    load_w(it * 2 + (N_FRONT + N_QK + b), b, it * (2 * P) + (COL_V + b * P))
            load_w(N_FRONT + N_QK + N_V, 0, COL_F, HEADS)

        @block.gpsimd
        def _(pool):
            nc.gpsimd.memset(taps[:, :, 0:1], 0.0).then_inc(taps_zeroed, 1)
            nc.gpsimd.memset(ident[:, :], 0.0).then_inc(consts_zero, 1)
            nc.gpsimd.memset(head_ones[:, :], 0.0).then_inc(consts_zero, 1)
            nc.gpsimd.memset(eps[:, :], RMS_EPS).then_inc(consts_ready, 1)
            wait(pool, consts_zero, 2)
            nc.gpsimd.affine_select(out=ident[:, :], in_=ident[:, :], compare_op=ALU.not_equal, fill=1.0,
                                    base=0, pattern=[[-1, P]], channel_multiplier=1).then_inc(consts_ready, 1)
            for half in range(2):
                s = slice(half * HD, (half + 1) * HD)
                wait(pool, consts_ready, 2 + half)
                nc.gpsimd.memset(head_ones[s, s], 1.0).then_inc(consts_ready, 1)
            pool.dma_start(bias[:, 0:20], b_in[0:COL_F].rearrange("(t p) -> p t", p=P),
                         allow_slow_non_contiguous=True).then_inc(param_loaded, 16)
            pool.dma_start(bias[:, 20:36], b_in[COL_G:].rearrange("(t p) -> p t", p=P),
                         allow_slow_non_contiguous=True).then_inc(param_loaded, 16)
            for half in range(2):
                for j, g in enumerate((q_norm_g, k_norm_g)):
                    pool.dma_start(gain_raw[half * HD:(half + 1) * HD, j:j + 1],
                                 g.rearrange("(p o) -> p o", o=1),
                         allow_slow_non_contiguous=True).then_inc(param_loaded, 16)
            pool.dma_start(conv_bias[:, :], dw_b.rearrange("(t p) -> p t", p=P),
                         allow_slow_non_contiguous=True).then_inc(param_loaded, 16)
            pool.dma_start(f_bias[:, 0:1], b_in[COL_F:COL_G].rearrange("(p o) -> p o", o=1),
                         allow_slow_non_contiguous=True).then_inc(param_loaded, 16)
            pool.dma_start(f_bias[:, 1:2], b_forget.rearrange("(p o) -> p o", o=1),
                         allow_slow_non_contiguous=True).then_inc(param_loaded, 16)
            wait(pool, taps_zeroed, 1)
            for t in range(CT):
                pool.dma_start(taps[:, t, 1:TAP_SLOTS],
                             dw_w[:, t * P:(t + 1) * P].rearrange("k p -> p k"),
                         allow_slow_non_contiguous=True).then_inc(param_loaded, 16)
            pool.sem_inc(w_split, 2)

            def split_w(n, b, loads, width=P):
                wait(pool, w_loaded[b], loads * 16)
                wait(pool, tile_done, n + 1)
                nc.gpsimd.tensor_copy(w_hi[:, b, :, 0:width], w_raw[:, b, :, 0:width]).then_inc(w_hi_ready, 1)
                wait(pool, w_hi_ready, n + 1)
                nc.gpsimd.tensor_tensor(w_lo[:, b, :, 0:width], w_raw[:, b, :, 0:width],
                                        raw(w_hi[:, b, :, 0:width]), ALU.subtract).then_inc(w_split, 1)

            with pool.Fori(0, CT) as ct:
                for j in range(6):
                    split_w(ct * 6 + j, j % 2, ct * 3 + (j // 2 + 1))
            with pool.Fori(0, N_QK // 2) as it:
                for b in range(2):
                    split_w(it * 2 + (N_FRONT + b), b, it + (N_FRONT // 2 + 1))
            with pool.Fori(0, N_V // 2) as it:
                for b in range(2):
                    split_w(it * 2 + (N_FRONT + N_QK + b), b, it + ((N_FRONT + N_QK) // 2 + 1))
            split_w(N_FRONT + N_QK + N_V, 0, (N_FRONT + N_QK + N_V) // 2 + 1, HEADS)

        @block.tensor
        def _(pe):
            pe.sem_inc(tile_done, 2)
            for s in bank_read:
                pe.sem_inc(s, 1)
            pe.wait_ge(consts_ready, 4)

            def turn_tokens(t, b, rows):
                pe.wait_ge(xn_ready, t + 3)
                pe.wait_ge(xn_lo_ready, t + 1)
                for c in range(DC):
                    m = nc.tensor.transpose(bank[:, 4 + 2 * b + c // 4, (c % 4) * P:(c % 4) * P + rows],
                                            work[0:rows, XN[b], c * P:(c + 1) * P], ident[0:rows, 0:rows])
                m.then_inc(xn_turned, 1)

            def project_rows(b, chunks, i, rows, width=P):
                at, size = chunks[i]
                for c in rows:
                    m = pair_matmuls(nc.tensor, bank[0:width, i, 0:size],
                                     (w_hi[:, b, c, 0:width], w_lo[:, b, c, 0:width]),
                                     (xnT_hi[:, c, at:at + size], xnT_lo[:, c, at:at + size]),
                                     c == 0, c == DC - 1)
                if c == DC - 1:
                    m.then_inc(chunk_done if i < len(chunks) - 1 else tile_done, 1)

            def project(n, b, chunks, uses, width=P, between=None):
                pe.wait_ge(w_split, n + 3)
                for i in range(len(chunks)):
                    pe.wait_ge(bank_read[i], uses[i == 4] + 1)
                    project_rows(b, chunks, i, range(DC), width)
                    if between:
                        between(i)

            with pe.Fori(0, 4) as it:
                for b in range(2):
                    turn_tokens(it * 2 + b, b, P)
            BESIDE = {8: (0, range(0, 3)), 9: (0, range(3, 6)), 10: (0, range(6, 8)),
                      11: (1, range(0, 3)), 12: (1, range(3, 6)), 13: (1, range(6, 8)),
                      14: (2, range(0, 4)), 15: (2, range(4, 8))}
            for t in range(8, NT):
                turn_tokens(t, t % 2, P)
                if t == 8:
                    pe.wait_ge(w_split, 3)
                i, rows = BESIDE[t]
                if rows[0] == 0:
                    pe.wait_ge(bank_read[i], 1)
                project_rows(0, LATER_FIRST, i, rows)
            turn_tokens(NT, 0, META)
            pe.wait_ge(xn_lo_ready, NT + 3)
            for i in (3, 4):
                pe.wait_ge(bank_read[i], 1)
                project_rows(0, LATER_FIRST, i, range(DC))

            def rest_of_front(ct):
                for j in range(1, 6):
                    project(ct * 6 + j, j % 2, FRONT_CHUNKS[j], (ct * 6 + j, ct * 2 + j))

            with pe.Fori(0, CT - 1) as ct:
                rest_of_front(ct)
                project(ct * 6 + 6, 0, FRONT_CHUNKS[0], (ct * 6 + 6, ct * 2 + 2))
            rest_of_front(CT - 1)

            def pair_tile(it, b):
                def head_sum(g):
                    i, r = g % 5, g % 2
                    size = CHUNKS[i][1]
                    pe.wait_ge(bank_read[i], it * 2 + ((N_FRONT if i < 4 else 2 * CT) + g // 5 + 2))
                    pe.wait_ge(root2_ready, it * 10 + (g + 1))
                    nc.tensor.matmul(bank[:, 5 + r, 0:size], head_ones[:, :], sq[:, r, 0:size],
                                     start=True, stop=True).then_inc(sum_ready, 1)

                first = isinstance(it, int) and it == 0 and b == 0
                project(it * 2 + (N_FRONT + b), b, CHUNKS, (it * 2 + (N_FRONT + b), it * 2 + (2 * CT + b)),
                        between=lambda i: None if first and i == 0 else head_sum(5 * b + i - 1))
                if isinstance(it, int) and it * 2 + b == N_QK - 1:
                    head_sum(9)

            over_pair_tiles(pe, pair_tile)
            with pe.Fori(0, N_V // 2) as it:
                for b in range(2):
                    project(it * 2 + (N_FRONT + N_QK + b), b, CHUNKS,
                            (it * 2 + (N_FRONT + N_QK + b), it * 2 + (2 * CT + N_QK + b)))
                    for i in range(5):
                        pe.wait_ge(bank_read[i], it * 2 + ((N_FRONT if i < 4 else 2 * CT) + N_QK + b + 2))
                    for g in range(5):
                        r = (5 * b + g) % 2
                        pe.wait_ge(v_lo_ready, it * 10 + (5 * b + g + 1))
                        for t in range(4 * g, min(4 * g + 4, KT)):
                            m = nc.tensor.transpose(bank[:, 5 + r, (t % 4) * P:(t % 4 + 1) * P],
                                                    work[:, 0, t * P:(t + 1) * P], ident[:, :])
                        m.then_inc(v_turned, 1)
            project(N_FRONT + N_QK + N_V, 0, CHUNKS,
                    (N_FRONT + N_QK + N_V, 2 * CT + N_QK + N_V), width=HEADS)

        @block.scalar
        def _(act):
            act.sem_inc(root2_ready, 2)
            wait(act, consts_ready, 4)

            def square_tokens(t, b, loads, rows):
                wait(act, x_loaded[b], loads * 16)
                nc.scalar.activation(work[0:rows, 2, D:2 * D], work[0:rows, XIN[b], 0:D], ACT.Square,
                                     accum_out=stat[0:rows, b, 0:1]).then_inc(squares_summed, 1)
                wait(act, var_ready, t + 1)
                nc.scalar.activation(stat[0:rows, b, 2:3], stat[0:rows, b, 1:2], ACT.Sqrt)\
                  .then_inc(root_ready, 1)

            def tokens_hi(t, b, rows):
                wait(act, xn_turned, t + 1)
                col = t * P + META if rows == P else 0
                nc.scalar.activation(xnT_hi[:, :, bass.ds(col, rows)],
                                     bank[:, 4 + 2 * b:6 + 2 * b, :].rearrange("p b (c t) -> p (b c) t", t=P)[:, :, 0:rows],
                                     ACT.Copy).then_inc(xn_hi_ready, 1)

            square_tokens(0, 0, 1, P)
            with act.Fori(0, NT // 2 - 1) as it:
                square_tokens(it * 2 + 1, 1, it + 1, P)
                tokens_hi(it * 2, 0, P)
                square_tokens(it * 2 + 2, 0, it + 2, P)
                tokens_hi(it * 2 + 1, 1, P)
            square_tokens(NT - 1, 1, NT // 2, P)
            tokens_hi(NT - 2, 0, P)
            square_tokens(NT, 0, NT // 2 + 1, META)
            tokens_hi(NT - 1, 1, P)
            tokens_hi(NT, 0, META)

            wait(act, params_ready, 1)
            with act.Fori(0, CT) as ct:
                for i, (at, size) in enumerate(LATER_FIRST):
                    wait_chunk(act, ct * 6, ct * FRONT_COUNT[6], i, LATER_FIRST)
                    nc.scalar.activation(work[:, 0, at:at + size], bank[:, i, 0:size], ACT.Sigmoid,
                                         bias=bias[:, bass.ds(ct + CT, 1)]).then_inc(bank_read[i], 1)
                for j in range(4):
                    b = j % 2
                    wait(act, gate_stored[b], ct * 32 + 16 * (j // 2 + 1))
                    for i in range(4):
                        wait_chunk(act, ct * 6 + (2 + j), ct * FRONT_COUNT[6] + FRONT_COUNT[2 + j], i, XCHUNKS)
                        nc.scalar.activation(work[:, 3 + b, 512 * i:512 * (i + 1)], bank[:, i, :],
                                             ACT.Sigmoid, bias=bias[:, bass.ds(ct * 4 + (20 + j), 1)])\
                          .then_inc(bank_read[i], 1)
                    for i in range(4):
                        wait(act, bank_read[i], ct * 6 + (2 + j + 2))
                    act.dma_start(gate_d[ct * 4 + j], work[:, 3 + b, 0:SEQ]).then_inc(gate_stored[b], 16)
                wait(act, tap_done, ct * (TAP_SLOTS + 1) + (TAP_SLOTS + 1))
                act.dma_start(conv_d[ct], work[:, 2, 0:SEQ]).then_inc(conv_stored, 16)

            for s in gate_stored:
                wait(act, s, 16 * (1 + 2 * CT))

            def pair_tile(it, b):
                def root_of(g):
                    r, size = g % 2, CHUNKS[g % 5][1]
                    wait(act, sum_ready, it * 10 + (g + 1))
                    wait(act, inv_ready, it * 10 + (g + 1))
                    nc.scalar.activation(root[:, r, 0:size], bank[:, 5 + r, 0:size], ACT.Sqrt,
                                         bias=eps[:, 0:1], scale=1.0 / HD).then_inc(root2_ready, 1)

                def high_of(g):
                    at, size = CHUNKS[g % 5]
                    wait(act, qn_ready, it * 10 + (g + 1))
                    nc.scalar.activation(work[:, 1 + 2 * (g // 5 % 2), at:at + size].bitcast(F32R),
                                         work[:, 0, at:at + size], ACT.Copy).then_inc(q_hi_ready, 1)

                first = isinstance(it, int) and it * 2 + b == 0
                last = isinstance(it, int) and it * 2 + b == N_QK - 1
                wait(act, qk_stored[b], it * 32 + 16)
                for i, (at, size) in enumerate(CHUNKS):
                    g = 5 * b + i
                    wait(act, q_lo_ready, it * 10 + (g + 1))
                    wait_chunk(act, it * 2 + (N_FRONT + b), it * 8 + (QK_COUNT + 4 * b), i, CHUNKS)
                    nc.scalar.activation(work[:, 0, at:at + size], bank[:, i, 0:size], ACT.Identity,
                                         bias=gain_bias[:, bass.ds(it * 2 + b, 1)],
                                         scale=gain[:, bass.ds(it * 2 + b, 1)])
                    nc.scalar.activation(sq[:, g % 2, 0:size], bank[:, i, 0:size], ACT.Square,
                                         bias=bias[:, bass.ds(it * 2 + (8 + b), 1)]).then_inc(bank_read[i], 1)
                    if i >= 1 or not first:
                        root_of(g - 1)
                    if i >= 2 or not first:
                        high_of(g - 2)
                if last:
                    root_of(9)
                    high_of(8)
                    high_of(9)

            over_pair_tiles(act, pair_tile)
            for s in qk_stored:
                wait(act, s, 16 + 16 * N_QK)
            wait(act, v_pad_ready, 1)
            with act.Fori(0, N_V // 2) as it:
                for b in range(2):
                    n = it * 2 + (N_FRONT + N_QK + b)
                    for i, (at, size) in enumerate(CHUNKS):
                        wait_chunk(act, n, it * 8 + (V_COUNT + 4 * b), i, CHUNKS)
                        nc.scalar.activation(work[:, 0, PAD + at:PAD + at + size], bank[:, i, 0:size],
                                             ACT.Identity, bias=bias[:, bass.ds(it * 2 + (16 + b), 1)])\
                          .then_inc(bank_read[i], 1)
                    wait(act, v_stored[b], it * 16 + 16)
                    for g in range(5):
                        r = (5 * b + g) % 2
                        tiles = min(4, KT - 4 * g)
                        wait(act, v_turned, it * 10 + (5 * b + g + 1))
                        nc.scalar.activation(
                            value_half(b, 4 * g, tiles, 0).bitcast(F32R),
                            bank[:, 5 + r, 0:tiles * P].rearrange("p (t h e) -> p t h e", h=2, e=HD),
                            ACT.Copy).then_inc(v_hi_ready, 1)
                    wait(act, v_lo_ready, it * 10 + (5 * b + 5 + 2))
                    act.dma_start(v_d[it * 2 + b], work[:, 1 + 2 * b:3 + 2 * b, :].rearrange("p s n -> p (s n)"))\
                       .then_inc(v_stored[b], 16)
            for s in v_stored:
                wait(act, s, 16 + 16 * (N_V // 2))

            wait(act, f_vec, 2)
            nc.scalar.activation(work[0:HEADS, 2, 0:L], work[0:HEADS, 1, 0:L], ACT.Exp, scale=-1.0)\
              .then_inc(f_act, 1)
            wait(act, f_act, 1)
            nc.scalar.activation(work[0:HEADS, 1, 0:L], work[0:HEADS, 2, 0:L], ACT.Ln, bias=1.0)\
              .then_inc(f_act, 1)
            wait(act, f_vec, 5)
            act.dma_start(decay_d, work[0:HEADS, 4, 0:L]).then_inc(decay_stored, 16)
            wait(act, decay_stored, 16)
            wait(act, conv_stored, 16 + 16 * CT)

        @block.vector
        def _(dve):
            dve.sem_inc(xn_ready, 2)
            dve.sem_inc(xn_lo_ready, 2)
            dve.wait_ge(norm_gain_loaded, 16)

            def scale_tokens(t, b, rows):
                s = stat[0:rows, b, :]
                dve.wait_ge(squares_summed, t + 1)
                nc.vector.tensor_scalar(s[:, 1:2], s[:, 0:1], 1.0 / D, RMS_EPS, ALU.mult, ALU.add)\
                  .then_inc(var_ready, 1)
                dve.wait_ge(root_ready, t + 1)
                nc.vector.reciprocal(s[:, 3:4], s[:, 2:3]).then_inc(newton_step, 1)
                dve.wait_ge(newton_step, t * 4 + 1)
                nc.vector.scalar_tensor_tensor(out=s[:, 4:5], in0=s[:, 3:4], scalar=s[:, 1:2], in1=s[:, 3:4],
                                               op0=ALU.mult, op1=ALU.mult).then_inc(newton_step, 1)
                dve.wait_ge(newton_step, t * 4 + 2)
                nc.vector.tensor_scalar(s[:, 5:6], s[:, 4:5], -0.5, 1.5, ALU.mult, ALU.add)\
                  .then_inc(newton_step, 1)
                dve.wait_ge(newton_step, t * 4 + 3)
                nc.vector.tensor_tensor(s[:, 6:7], s[:, 5:6], s[:, 3:4], ALU.mult).then_inc(newton_step, 1)
                dve.wait_ge(newton_step, t * 4 + 4)
                nc.vector.scalar_tensor_tensor(out=work[0:rows, XN[b], 0:D], in0=work[0:rows, XIN[b], 0:D],
                                               scalar=s[:, 6:7], in1=work[0:rows, 2, 0:D],
                                               op0=ALU.mult, op1=ALU.mult).then_inc(xn_ready, 1)

            def tokens_lo(t, b, rows):
                dve.wait_ge(xn_hi_ready, t + 1)
                dst = bass.ds(t * P + META if rows == P else 0, rows)
                nc.vector.tensor_tensor(xnT_lo[:, :, dst],
                                        bank[:, 4 + 2 * b:6 + 2 * b, :].rearrange("p b (c t) -> p (b c) t", t=P)[:, :, 0:rows],
                                        raw(xnT_hi[:, :, dst]), ALU.subtract).then_inc(xn_lo_ready, 1)

            scale_tokens(0, 0, P)
            with dve.Fori(0, NT // 2 - 1) as it:
                scale_tokens(it * 2 + 1, 1, P)
                tokens_lo(it * 2, 0, P)
                dve.wait_ge(xn_turned, it * 2 + 1)
                scale_tokens(it * 2 + 2, 0, P)
                tokens_lo(it * 2 + 1, 1, P)
            scale_tokens(NT - 1, 1, P)
            tokens_lo(NT - 2, 0, P)
            scale_tokens(NT, 0, META)
            tokens_lo(NT - 1, 1, P)
            tokens_lo(NT, 0, META)

            dve.wait_ge(param_loaded, 16 * 13)
            for t in range(8):
                nc.vector.tensor_scalar(gain[:, t:t + 1], gain_raw[:, t // 4:t // 4 + 1],
                                        HD ** -0.5 if t < 4 else 1.0, None, ALU.mult).then_inc(setup_step, 1)
            dve.wait_ge(setup_step, 8)
            nc.vector.tensor_tensor(gain_bias[:, :], gain[:, :], bias[:, 8:16], ALU.mult).then_inc(setup_step, 1)
            nc.vector.tensor_tensor(f_bias[:, 2:3], f_bias[:, 0:1], f_bias[:, 1:2], ALU.add).then_inc(setup_step, 1)
            nc.vector.memset(work[:, 1, 0:TAPS - 1], 0.0).then_inc(setup_step, 1)
            dve.wait_ge(setup_step, 11)
            dve.sem_inc(params_ready, 1)
            dve.sem_inc(conv_stored, 16)
            dve.sem_inc(gate_stored[0], 16)
            dve.sem_inc(gate_stored[1], 16)

            with dve.Fori(0, CT) as ct:
                for i, (at, size) in enumerate(LATER_FIRST):
                    wait_chunk(dve, ct * 6 + 1, ct * FRONT_COUNT[6] + FRONT_COUNT[1], i, LATER_FIRST)
                    nc.vector.scalar_tensor_tensor(out=work[:, 1, TAPS - 1 + at:TAPS - 1 + at + size],
                                                   in0=bank[:, i, 0:size], scalar=bias[:, bass.ds(ct, 1)],
                                                   in1=work[:, 0, at:at + size], op0=ALU.add, op1=ALU.mult)\
                      .then_inc(bank_read[i], 1)
                for i in range(5):
                    dve.wait_ge(bank_read[i], (ct * 6 if i < 4 else ct * 2) + 3)
                base = ct * (TAP_SLOTS + 1)
                dve.wait_ge(conv_stored, ct * 16 + 16)
                nc.vector.tensor_scalar(work[:, 2, 0:SEQ], work[:, 1, META:META + SEQ], 0.0,
                                        conv_bias[:, bass.ds(ct, 1)], ALU.mult, ALU.add).then_inc(tap_done, 1)
                for q in range(TAP_SLOTS):
                    dve.wait_ge(tap_done, base + (q + 1))
                    nc.vector.scalar_tensor_tensor(out=work[:, 2, 0:SEQ],
                                                   in0=work[:, 1, META - 1 + q:META - 1 + q + SEQ],
                                                   scalar=taps[:, bass.ds(ct, 1), q],
                                                   in1=work[:, 2, 0:SEQ], op0=ALU.mult, op1=ALU.add)\
                      .then_inc(tap_done, 1)

            for s in gate_stored:
                dve.wait_ge(s, 16 * (1 + 2 * CT))
            dve.wait_ge(conv_stored, 16 + 16 * CT)
            dve.sem_inc(inv_ready, 2)
            dve.sem_inc(q_lo_ready, 5)
            dve.sem_inc(qk_stored[0], 16)
            dve.sem_inc(qk_stored[1], 16)


            def pair_tile(it, b):
                def low_of(g):
                    at, size = CHUNKS[g % 5]
                    slot = 1 + 2 * (g // 5 % 2)
                    dve.wait_ge(q_hi_ready, it * 10 + (g + 1))
                    nc.vector.tensor_tensor(work[:, slot + 1, at:at + size].bitcast(F32R),
                                            work[:, 0, at:at + size], work[:, slot, at:at + size],
                                            ALU.subtract).then_inc(q_lo_ready, 1)

                dve.wait_ge(qk_stored[b], it * 32 + 16)
                for i, (at, size) in enumerate(CHUNKS):
                    g = 5 * b + i
                    r = g % 2
                    dve.wait_ge(root2_ready, it * 10 + (g + 3))
                    nc.vector.reciprocal(inv_root[:, r, 0:size], root[:, r, 0:size]).then_inc(inv_ready, 1)
                    dve.wait_ge(inv_ready, it * 10 + (g + 3))
                    nc.vector.tensor_tensor(work[:, 0, at:at + size], work[:, 0, at:at + size],
                                            inv_root[:, r, 0:size], ALU.mult).then_inc(qn_ready, 1)
                    if i >= 1 or not (isinstance(it, int) and it * 2 + b == 0):
                        low_of(g - 1)
                if isinstance(it, int) and it * 2 + b == N_QK - 1:
                    low_of(9)

            over_pair_tiles(dve, pair_tile)
            for s in qk_stored:
                dve.wait_ge(s, 16 + 16 * N_QK)
            dve.wait_ge(q_lo_ready, 5 * N_QK + 5)
            nc.vector.memset(work[:, 0, 0:PAD], 0.0).then_inc(v_pad_ready, 1)
            dve.sem_inc(v_lo_ready, 2)
            dve.sem_inc(v_stored[0], 16)
            dve.sem_inc(v_stored[1], 16)

            with dve.Fori(0, N_V // 2) as it:
                for b in range(2):
                    for g in range(5):
                        tiles = min(4, KT - 4 * g)
                        r = (5 * b + g) % 2
                        dve.wait_ge(v_hi_ready, it * 10 + (5 * b + g + 1))
                        nc.vector.tensor_tensor(
                            value_half(b, 4 * g, tiles, 1).bitcast(F32R),
                            bank[:, 5 + r, 0:tiles * P].rearrange("p (t h e) -> p t h e", h=2, e=HD),
                            value_half(b, 4 * g, tiles, 0), ALU.subtract).then_inc(v_lo_ready, 1)

            for s in v_stored:
                dve.wait_ge(s, 16 + 16 * (N_V // 2))
            for i, (at, size) in enumerate(CHUNKS):
                wait_chunk(dve, N_FRONT + N_QK + N_V, F_COUNT, i, CHUNKS)
                m = nc.vector.tensor_scalar(work[0:HEADS, 0, at:at + size], bank[0:HEADS, i, 0:size],
                                            f_bias[:, 2:3], None, ALU.add)
            m.then_inc(f_vec, 1)
            dve.wait_ge(f_vec, 1)
            nc.vector.scalar_tensor_tensor(out=work[0:HEADS, 1, 0:L], in0=work[0:HEADS, 0, 0:L], scalar=-1.0,
                                           in1=work[0:HEADS, 0, 0:L], op0=ALU.mult, op1=ALU.max)\
              .then_inc(f_vec, 1)
            dve.wait_ge(f_act, 2)
            nc.vector.scalar_tensor_tensor(out=work[0:HEADS, 3, 0:L], in0=work[0:HEADS, 0, 0:L], scalar=0.0,
                                           in1=work[0:HEADS, 1, 0:L], op0=ALU.min, op1=ALU.subtract)\
              .then_inc(f_vec, 1)
            nc.vector.memset(work[0:HEADS, 2, 0:L], 1.0).then_inc(f_vec, 1)
            dve.wait_ge(f_vec, 4)
            nc.vector.tensor_tensor_scan(work[0:HEADS, 4, 0:L], work[0:HEADS, 2, 0:L], work[0:HEADS, 3, 0:L],
                                         0.0, ALU.mult, ALU.subtract).then_inc(f_vec, 1)

def stage_attend(nc, qk_d, v_d, decay_d, o_d, inv_d):
    with ExitStack() as ctx:
        def sb(name, shape, dt=F32):
            return ctx.enter_context(nc.sbuf_tensor("attend_" + name, shape, dt))

        def sem(name):
            return ctx.enter_context(nc.semaphore("attend_" + name))

        wait = register_waits(sem)

        ORDER = [i for j in range(NT // 2) for i in (NT - 1 - j, j)]
        UNITS = 2 * NT
        TILE = [ORDER[u % NT] for u in range(UNITS)]
        N_GROUP = [-(-(i + 2) // 4) for i in TILE]
        FIRST = [sum(N_GROUP[:u]) for u in range(UNITS + 1)]
        PAIR_GROUPS = FIRST[-1]
        AHEAD = 3
        LAG = 2
        BUF = 4
        GROUP = [(u, g) for u in range(UNITS) for g in range(N_GROUP[u])]

        keys = sb("keys", [P, 2, L], F32R)
        q_hi = sb("q_hi", [P, 2, SEQ], F32R)
        q_lo = sb("q_lo", [P, 2, SEQ], F32R)
        values = sb("values", [P, 2, KT, P], F32R)
        decay = sb("decay", [P, 2, L])
        scores = sb("scores", [P, BUF // 2, KCOLS])
        probs = sb("probs", [P, BUF, KCOLS])
        low = sb("low", [P, 4, 5])
        row_sum = sb("row_sum", [P, PAIRS * UNITS])
        inv_sum = sb("inv_sum", [P, PAIRS * UNITS])
        inv_rows = sb("inv_rows", [P, P])
        pT = sb("pT", [P, 3, 4, 2, P], F32R)
        o_raw = sb("o_raw", [P, 2, 512])
        o_sb = sb("o_sb", [P, 2, SEQ])
        ident = sb("ident", [P, P])
        ident16 = sb("ident16", [P, P], BF16)
        mask = sb("mask", [P, P], BF16)
        s_bank = ctx.enter_context(nc.psum_tensor("attend_s_bank", [P, 3, 512], F32))
        t_bank = ctx.enter_context(nc.psum_tensor("attend_t_bank", [P, 3, 512], F32))
        o_bank = ctx.enter_context(nc.psum_tensor("attend_o_bank", [P, 2, 512], F32))

        consts_ready = sem("consts_ready")
        head_loaded = [sem("head_loaded0"), sem("head_loaded1")]
        values_loaded = [sem("values_loaded0"), sem("values_loaded1")]
        s_done = sem("s_done")
        s_read = sem("s_read")
        exp_done = sem("exp_done")
        turned = sem("turned")
        hi_done = sem("hi_done")
        lo_done = sem("lo_done")
        pv_done = sem("pv_done")
        o_read = sem("o_read")
        o_added = sem("o_added")
        inv_done = sem("inv_done")
        o_stored = [sem("o_stored0"), sem("o_stored1")]
        inv_stored = sem("inv_stored")

        block = ctx.enter_context(nc.Block())

        def before(it, j):
            return it * PAIR_GROUPS + (max(0, j - 2) + 1)

        def over_pairs(eng, start, pair):
            start()
            with eng.Fori(0, PAIRS - 1) as it:
                pair(it, True)
            pair(PAIRS - 1, False)

        def later(it, u, ahead, more):
            if u + ahead < UNITS:
                return it, u + ahead
            return (it + 1, u + ahead - UNITS) if more else (it, None)

        def columns(u, g):
            a = max(PAD, 512 * g)
            e = min(512 * (g + 1), (TILE[u] + 2) * P)
            return a, e, a - 512 * g, e - 512 * g

        @block.sync
        def _(sp):
            def load_head(it, h):
                wait(sp, o_read, it * 16 + (8 * h + 8))
                rows = slice(h * HD, (h + 1) * HD)
                for half in range(2):
                    part = slice(half * HD, (half + 1) * HD)
                    sp.dma_start(raw(keys[part, h, :]), qk_d[it + PAIRS, half, rows, :])\
                      .then_inc(head_loaded[h], 16)
                    sp.dma_start(raw(q_hi[part, h, :]), qk_d[it, 0, rows, META:L])\
                      .then_inc(head_loaded[h], 16)
                    sp.dma_start(raw(q_lo[part, h, :]), qk_d[it, 1, rows, META:L])\
                      .then_inc(head_loaded[h], 16)
                sp.dma_start(decay[:, h, :], decay_d[bass.ds(it * 2 + h, 1), :].to_broadcast([P, L]))\
                  .then_inc(head_loaded[h], 16)
                sp.dma_start(raw(values[:, h, :, :]),
                             v_d[it].rearrange("p (t h n) -> p h t n", h=2, n=P)[:, h])\
                  .then_inc(values_loaded[h], 16)

            with sp.Fori(0, PAIRS) as it:
                load_head(it, 0)
                load_head(it, 1)

        @block.gpsimd
        def _(pool):
            nc.gpsimd.memset(ident[:, :], 0.0).then_inc(consts_ready, 1)
            wait(pool, consts_ready, 1)
            nc.gpsimd.affine_select(out=ident[:, :], in_=ident[:, :], compare_op=ALU.not_equal, fill=1.0,
                                    base=0, pattern=[[-1, P]], channel_multiplier=1).then_inc(consts_ready, 1)
            wait(pool, consts_ready, 2)
            nc.gpsimd.tensor_copy(ident16[:, :], ident[:, :]).then_inc(consts_ready, 1)
            wait(pool, consts_ready, 3)
            nc.gpsimd.memset(mask[:, :], 0.0).then_inc(consts_ready, 1)
            wait(pool, consts_ready, 4)
            nc.gpsimd.affine_select(out=mask[:, :], in_=mask[:, :], compare_op=ALU.is_ge, fill=-1e30,
                                    base=0, pattern=[[-1, P]], channel_multiplier=1).then_inc(consts_ready, 1)
            wait(pool, consts_ready, 5)
            nc.gpsimd.memset(probs[:, :, 0:PAD], 0.0).then_inc(consts_ready, 1)
            pool.sem_inc(o_added, 4)
            with pool.Fori(0, PAIRS) as it:
                for u in range(UNITS):
                    h, m = u // NT, u // 2
                    if u % 2 == 0:
                        wait(pool, o_read, it * 16 + (m + 17))
                    i = TILE[u]
                    r = o_raw[:, m % 2, 2 * P * (u % 2):2 * P * (u % 2 + 1)]
                    nc.gpsimd.tensor_tensor(o_sb[:, h, i * P:(i + 1) * P], r[:, 0:P], r[:, P:2 * P],
                                            ALU.add).then_inc(o_added, 1)
                    if u % NT == NT - 1:
                        wait(pool, o_added, it * UNITS + (u + 5))
                        pool.dma_start(o_d[it * 2 + h], o_sb[:, h, :]).then_inc(o_stored[h], 16)
                for s in o_stored:
                    wait(pool, s, it * 16 + 16)
            wait(pool, inv_done, 3)
            pool.dma_start(inv_d.rearrange("h (t q) -> (h t) q", q=P), inv_rows[:, :]).then_inc(inv_stored, 16)
            wait(pool, inv_stored, 16)

        @block.tensor
        def _(pe):
            pe.sem_inc(turned, 1)
            pe.sem_inc(pv_done, 1)
            pe.wait_ge(consts_ready, 6)

            def score(it, u, g):
                h, j = u // NT, FIRST[u] + g
                if u % NT == 0 and g == 0:
                    pe.wait_ge(head_loaded[h], it * 112 + 112)
                pe.wait_ge(s_read, before(it, j))
                a, e, ba, be = columns(u, g)
                out = s_bank[:, j % 3, ba:be]
                qs = slice(TILE[u] * P, TILE[u] * P + P)
                nc.tensor.matmul(out, q_hi[:, h, qs], keys[:, h, a - PAD:e - PAD], start=True, stop=False)
                if g == N_GROUP[u] - 1:
                    nc.tensor.matmul(s_bank[:, j % 3, be - P:be], ident16[:, :], mask[:, :],
                                     start=False, stop=False)
                nc.tensor.matmul(out, q_lo[:, h, qs], keys[:, h, a - PAD:e - PAD],
                                 start=False, stop=True).then_inc(s_done, 1)

            def turn(it, u, g):
                j = FIRST[u] + g
                if g == 0:
                    pe.wait_ge(exp_done, it * UNITS + (u + 3))
                pe.wait_ge(lo_done, before(it, j))
                for t in range(4 * g, min(4 * g + 4, TILE[u] + 2)):
                    m = nc.tensor.transpose(t_bank[:, j % 3, (t % 4) * P:(t % 4 + 1) * P],
                                            probs[:, u % BUF, t * P:(t + 1) * P], ident[:, :])
                m.then_inc(turned, 1)

            def times_values(it, u, g):
                h, j = u // NT, FIRST[u] + g
                if u % NT == 0 and g == 0:
                    pe.wait_ge(values_loaded[h], it * 16 + 16)
                if u % 2 == 0 and g == 0:
                    pe.wait_ge(o_read, it * 16 + (u // 2 + 15))
                pe.wait_ge(lo_done, it * PAIR_GROUPS + (j + 2))
                out = o_bank[:, (u // 2) % 2, (u % 2) * 2 * P:(u % 2 + 1) * 2 * P]
                last = TILE[u] + 1
                for t in range(4 * g, min(4 * g + 4, last + 1)):
                    m = nc.tensor.matmul(out, values[:, h, t, :],
                                         pT[:, j % 3, t % 4].rearrange("p k q -> p (k q)"),
                                         start=t == 0, stop=t == last)
                m.then_inc(pv_done, 1)

            def start():
                for u in range(AHEAD):
                    for g in range(N_GROUP[u]):
                        score(0, u, g)

            def pair(it, more):
                for j, (u, g) in enumerate(GROUP):
                    to, next_u = later(it, u, AHEAD, more)
                    if next_u is not None and g < N_GROUP[next_u]:
                        score(to, next_u, g)
                    turn(it, u, g)
                    if next_u is not None and g == N_GROUP[u] - 1:
                        for rest in range(g + 1, N_GROUP[next_u]):
                            score(to, next_u, rest)
                    if j >= LAG:
                        times_values(it, *GROUP[j - LAG])
                for j in range(PAIR_GROUPS - LAG, PAIR_GROUPS):
                    times_values(it, *GROUP[j])

            over_pairs(pe, start, pair)
            pe.wait_ge(inv_done, 1)
            pe.wait_ge(lo_done, PAIRS * PAIR_GROUPS + 1)
            nc.tensor.transpose(t_bank[:, 0, 0:P], inv_sum[:, :], ident[:, :]).then_inc(inv_done, 1)

        @block.scalar
        def _(act):
            act.sem_inc(exp_done, 2)
            act.sem_inc(o_read, 16)
            wait(act, consts_ready, 6)
            def exponentials(it, u):
                last = N_GROUP[u] - 1
                act.wait_ge(s_read, it * PAIR_GROUPS + (FIRST[u + 1] + 1))
                if u >= BUF:
                    wait(act, turned, it * PAIR_GROUPS + (FIRST[u - BUF + 1] + 1))
                elif u >= 2 or isinstance(it, int):
                    wait(act, turned, it * PAIR_GROUPS + 1)
                else:
                    wait(act, turned, it * PAIR_GROUPS + (FIRST[UNITS + u - BUF + 1] - PAIR_GROUPS + 1))
                e = (TILE[u] + 2) * P
                nc.scalar.activation(probs[:, u % BUF, PAD:e], scores[:, u % 2, PAD:e], ACT.Exp,
                                     bias=low[:, u % 4, last:last + 1], scale=-1.0,
                                     accum_out=row_sum[:, bass.ds(it * UNITS + (u // NT * NT + TILE[u]), 1)]).then_inc(exp_done, 1)

            def high(it, u, g):
                j = FIRST[u] + g
                n = min(4, TILE[u] + 2 - 4 * g)
                act.wait_ge(pv_done, before(it, j))
                wait(act, turned, it * PAIR_GROUPS + (j + 2))
                nc.scalar.activation(pT[:, j % 3, 0:n, 0, :],
                                     t_bank[:, j % 3, 0:n * P].rearrange("p (t q) -> p t q", q=P), ACT.Copy)\
                  .then_inc(hi_done, 1)

            def take_output(it, m):
                act.wait_ge(o_added, it * UNITS + (2 * m + 2))
                wait(act, pv_done, it * PAIR_GROUPS + (FIRST[2 * m + 2] + 1))
                nc.scalar.activation(o_raw[:, m % 2, :], o_bank[:, m % 2, :], ACT.Copy).then_inc(o_read, 1)

            def start():
                exponentials(0, 0)
                exponentials(0, 1)

            def pair(it, more):
                for u, g in GROUP:
                    high(it, u, g)
                    to, next_u = later(it, u, 2, more)
                    if g == N_GROUP[u] // 2 and next_u is not None:
                        exponentials(to, next_u)
                    if g == 0 and u % 2 == 1 and u >= 3:
                        take_output(it, (u - 3) // 2)
                take_output(it, UNITS // 2 - 1)

            over_pairs(act, start, pair)

        @block.vector
        def _(dve):
            dve.sem_inc(s_read, 1)
            dve.sem_inc(lo_done, 1)
            def take_scores(it, u, g):
                h, j = u // NT, FIRST[u] + g
                if u % NT == 0 and g == 0:
                    dve.wait_ge(head_loaded[h], it * 112 + 112)
                if g == 0:
                    dve.wait_ge(exp_done, it * UNITS + (u + 1))
                else:
                    dve.wait_ge(s_read, it * PAIR_GROUPS + (j + 1))
                wait(dve, s_done, it * PAIR_GROUPS + (j + 1))
                a, e, ba, be = columns(u, g)
                nc.vector.tensor_tensor_reduce(scores[:, u % 2, a:e], s_bank[:, j % 3, ba:be],
                                               decay[:, h, a - PAD:e - PAD], -1.0,
                                               low[:, u % 4, g - 1:g] if g else 1e38,
                                               ALU.add, ALU.min, low[:, u % 4, g:g + 1]).then_inc(s_read, 1)

            def low_part(it, u, g):
                j = FIRST[u] + g
                n = min(4, TILE[u] + 2 - 4 * g)
                dve.wait_ge(hi_done, it * PAIR_GROUPS + (j + 1))
                nc.vector.tensor_tensor(pT[:, j % 3, 0:n, 1, :],
                                        t_bank[:, j % 3, 0:n * P].rearrange("p (t q) -> p t q", q=P),
                                        raw(pT[:, j % 3, 0:n, 0, :]), ALU.subtract).then_inc(lo_done, 1)

            def start():
                for u in range(AHEAD):
                    for g in range(N_GROUP[u]):
                        take_scores(0, u, g)

            def pair(it, more):
                for u, g in GROUP:
                    to, next_u = later(it, u, AHEAD, more)
                    if next_u is not None and g < N_GROUP[next_u]:
                        take_scores(to, next_u, g)
                    low_part(it, u, g)
                    if next_u is not None and g == N_GROUP[u] - 1:
                        for rest in range(g + 1, N_GROUP[next_u]):
                            take_scores(to, next_u, rest)

            over_pairs(dve, start, pair)
            dve.wait_ge(exp_done, PAIRS * UNITS + 2)
            nc.vector.reciprocal(inv_sum[:, :], row_sum[:, :]).then_inc(inv_done, 1)
            dve.wait_ge(inv_done, 2)
            nc.vector.tensor_copy(inv_rows[:, :], t_bank[:, 0, 0:P]).then_inc(inv_done, 1)

def stage_merge(nc, conv_ln_g, conv_ln_b, w_conv_out, b_conv_out, w_attn_out,
                conv_d, gate_d, o_d, inv_d, merged_d):
    TC = SEQ // 512
    W_CHUNKS = 2 * CT
    with ExitStack() as ctx:
        def sb(name, shape, dt=F32):
            return ctx.enter_context(nc.sbuf_tensor("merge_" + name, shape, dt))

        def sem(name):
            return ctx.enter_context(nc.semaphore("merge_" + name))

        wait = register_waits(sem)

        w_raw = sb("wm_raw", [P, 2, D])
        w_hi = sb("wm_hi", [P, W_CHUNKS, D], F32R)
        w_lo = sb("wm_lo", [P, W_CHUNKS, D], F32R)
        in_hi = sb("in_hi", [P, 2, W_CHUNKS, 512], F32R)
        in_lo = sb("in_lo", [P, 2, W_CHUNKS, 512], F32R)
        conv = sb("conv", [P, CT, 512])
        centred_sb = sb("centred_sb", [P, CT, 512])
        root = sb("ln_root", [P, 512])
        inv_root = sb("ln_inv_root", [P, 512])
        o_top = sb("o_top", [P, PAIRS, 512])
        o_low = sb("o_low", [P, PAIRS, 512])
        o_inv = sb("o_inv", [P, PAIRS, 512])
        gates = sb("gates", [P, 2, 2, 512])
        prod_c = sb("prod_c", [P, 2, 512])
        prod_a = sb("prod_a", [P, 2, 512])
        m_pair = sb("m_pair", [P, 2, 2, 512])
        mean_w = sb("mean_w", [P, P])
        eps = sb("ln_eps", [P, 1])
        ln = sb("ln", [P, 2, CT])
        b_out = sb("b_out", [P, DC])
        stat_bank = ctx.enter_context(nc.psum_tensor("merge_stat_bank", [P, 2, 512], F32))
        y_bank = ctx.enter_context(nc.psum_tensor("merge_y_bank", [P, 2, 2, 512], F32))

        consts_ready = sem("consts_ready")
        param_loaded = sem("param_loaded")
        w_loaded = [sem(f"w_loaded{i}") for i in range(2)]
        w_hi_ready = sem("w_hi_ready")
        w_ready = sem("w_ready")
        conv_loaded = sem("conv_loaded")
        o_loaded = sem("o_loaded")
        mean_done = sem("mean_done")
        centred = sem("centred")
        squared = sem("squared")
        var_done = sem("var_done")
        ln_root_ready = sem("ln_root_ready")
        ln_inv_ready = sem("ln_inv_ready")
        ln_scaled = sem("ln_scaled")
        silu_done = sem("silu_done")
        s_hi_ready = sem("s_hi_ready")
        s_lo_ready = sem("s_lo_ready")
        o_step = sem("o_step")
        gates_loaded = [sem("gates_loaded0"), sem("gates_loaded1")]
        y_done = sem("y_done")
        y_taken = sem("y_taken")
        merged = sem("merged")
        m_hi_ready = sem("m_hi_ready")
        m_lo_ready = sem("m_lo_ready")
        m_stored = [sem("m_stored0"), sem("m_stored1")]

        block = ctx.enter_context(nc.Block())

        def over_chunks(eng, prepare, product):
            with eng.Fori(0, TC - 1) as c:
                for t in range(DC):
                    product(c, t)
                    prepare(c + 1, t)
            for t in range(DC):
                product(TC - 1, t)

        def prepare_heads(eng, c, piece):
            step, half = piece // 2, piece % 2
            s = slice(2 * half, 2 * half + 2)
            d = slice(CT + 2 * half, CT + 2 * half + 2)
            if piece == 0:
                wait(eng, o_loaded, c * 96 + 96)
            wait(eng, o_step, c * 8 + (8 + piece))
            if step == 0:
                m = eng.tensor_tensor(o_top[:, s, :], o_top[:, s, :], o_low[:, s, :], ALU.add)
            elif step == 1:
                m = eng.tensor_tensor(o_top[:, s, :], o_top[:, s, :], o_inv[:, s, :], ALU.mult)
            elif step == 2:
                m = eng.activation(in_hi[:, c & 1, d, :], o_top[:, s, :], ACT.Copy)
            else:
                m = eng.tensor_tensor(in_lo[:, c & 1, d, :], o_top[:, s, :], raw(in_hi[:, c & 1, d, :]),
                                      ALU.subtract)
            m.then_inc(o_step, 1)

        @block.sync
        def _(sp):
            def load_conv(c):
                wait(sp, s_lo_ready, c + 1)
                sp.dma_start(conv[:, :, :], conv_d[:, :, bass.ds(c * 512, 512)].rearrange("t p n -> p t n"))\
                  .then_inc(conv_loaded, 16)

            def load_heads(c):
                wait(sp, o_step, c * 8 + 8)
                cols = bass.ds(c * 512, 512)
                for h in range(2):
                    part = slice(h * HD, (h + 1) * HD)
                    heads = o_d.rearrange("(t h) (k e) n -> h k e t n", h=2, k=2)
                    sp.dma_start(o_top[part, :, :], heads[h, 0][:, :, cols]).then_inc(o_loaded, 16)
                    sp.dma_start(o_low[part, :, :], heads[h, 1][:, :, cols]).then_inc(o_loaded, 16)
                    rows = inv_d.rearrange("(o t h) n -> h o t n", h=2, o=1)[h][:, :, cols]
                    sp.dma_start(o_inv[part, :, :], rows.to_broadcast([HD, PAIRS, 512])).then_inc(o_loaded, 16)

            def load_gates(c, t):
                wait(sp, y_taken, c * (2 * DC) + (2 * t + 2))
                for k in range(2):
                    sp.dma_start(gates[:, t % 2, k, :], gate_d[k * DC + t, :, bass.ds(c * 512, 512)])\
                      .then_inc(gates_loaded[t % 2], 16)

            def store(c, t):
                wait(sp, m_lo_ready, c * DC + (t + 3))
                for half in range(2):
                    sp.dma_start(merged_d[bass.ds(c * 4, 4), :, t, half, :].rearrange("j p n -> p j n"),
                                 m_pair[:, t % 2, half, :].rearrange("p (j n) -> p j n", n=P))\
                      .then_inc(m_stored[t % 2], 16)

            load_conv(0)
            for k in range(W_CHUNKS):
                w, c = (w_conv_out, k) if k < CT else (w_attn_out, k - CT)
                if k >= 2:
                    wait(sp, w_ready, k - 1)
                if k == CT:
                    load_heads(0)
                sp.dma_start(w_raw[:, k % 2, :], w[c * P:(c + 1) * P, :]).then_inc(w_loaded[k % 2], 16)
                if k == 0:
                    for j, g in enumerate((conv_ln_g, conv_ln_b)):
                        sp.dma_start(ln[:, j, :], g.rearrange("(t p) -> p t", p=P),
                                     allow_slow_non_contiguous=True).then_inc(param_loaded, 16)
                    sp.dma_start(b_out[:, :], b_conv_out.rearrange("(t p) -> p t", p=P),
                                 allow_slow_non_contiguous=True).then_inc(param_loaded, 16)

            load_gates(0, 0)
            load_gates(0, 1)
            load_conv(1)
            load_heads(1)

            def chunk(c, next_chunks):
                for t in range(DC):
                    store(c, t)
                    if t + 2 < DC:
                        load_gates(c, t + 2)
                    elif next_chunks >= 1:
                        load_gates(c + 1, t + 2 - DC)
                    if t == 5 and next_chunks == 2:
                        load_conv(c + 2)
                if next_chunks == 2:
                    load_heads(c + 2)

            with sp.Fori(0, TC - 2) as c:
                chunk(c, 2)
            chunk(TC - 2, 1)
            chunk(TC - 1, 0)
            for s in m_stored:
                wait(sp, s, 32 + 16 * TC * DC)

        @block.gpsimd
        def _(pool):
            nc.gpsimd.memset(mean_w[:, :], 1.0 / CW).then_inc(consts_ready, 1)
            nc.gpsimd.memset(eps[:, :], LN_EPS).then_inc(consts_ready, 1)
            pool.sem_inc(o_step, 8)
            pool.sem_inc(m_lo_ready, 2)

            def prepare(c, piece):
                if piece == 5:
                    prepare_heads(pool, c, 6)
                    prepare_heads(pool, c, 7)

            def product(c, t):
                b = t % 2
                wait(pool, m_hi_ready, c * DC + (t + 1))
                nc.gpsimd.tensor_tensor(m_pair[:, b, 1, :].bitcast(F32R), prod_c[:, b, :], m_pair[:, b, 0, :],
                                        ALU.subtract).then_inc(m_lo_ready, 1)

            prepare(0, 5)
            over_chunks(pool, prepare, product)

        @block.tensor
        def _(pe):
            pe.wait_ge(consts_ready, 2)

            def prepare(c, piece):
                if piece == 0:
                    pe.wait_ge(conv_loaded, c * 16 + 16)
                    src, done = conv, mean_done
                elif piece == 2:
                    pe.wait_ge(squared, c + 1)
                    src, done = conv, var_done
                else:
                    return
                for t in range(CT):
                    m = nc.tensor.matmul(stat_bank[:, piece // 2, :], mean_w[:, :], src[:, t, :],
                                         start=t == 0, stop=t == CT - 1)
                m.then_inc(done, 1)

            def product(c, t):
                if t == 0:
                    pe.wait_ge(w_ready, CT)
                    pe.wait_ge(s_lo_ready, c + 2)
                for k in range(2):
                    if t == 0 and k == 1:
                        pe.wait_ge(w_ready, W_CHUNKS)
                        pe.wait_ge(o_step, c * 8 + 16)
                    pe.wait_ge(y_taken, c * (2 * DC) + (2 * t + k + 1))
                    for i in range(CT):
                        r = k * CT + i
                        cols = slice(t * P, (t + 1) * P)
                        m = pair_matmuls(nc.tensor, y_bank[:, t % 2, k, :], (w_hi[:, r, cols], w_lo[:, r, cols]),
                                         (in_hi[:, c & 1, r, :], in_lo[:, c & 1, r, :]), i == 0, i == CT - 1)
                    m.then_inc(y_done, 1)

            prepare(0, 0)
            prepare(0, 2)
            over_chunks(pe, prepare, product)

        @block.scalar
        def _(act):
            for s in m_stored:
                act.sem_inc(s, 32)

            def high(k):
                wait(act, w_loaded[k % 2], 16 * (k // 2 + 1))
                nc.scalar.activation(w_hi[:, k, :], w_raw[:, k % 2, :], ACT.Copy).then_inc(w_hi_ready, 1)

            wait(act, consts_ready, 2)
            wait(act, param_loaded, 48)

            def prepare(c, piece, overlapped=True):
                if piece == 1:
                    wait(act, centred, c + 1)
                    nc.scalar.activation(conv[:, :, :], centred_sb[:, :, :], ACT.Square).then_inc(squared, 1)
                elif piece == 2:
                    wait(act, var_done, c + 1)
                    nc.scalar.activation(root[:, :], stat_bank[:, 1, :], ACT.Sqrt, bias=eps[:, 0:1])\
                      .then_inc(ln_root_ready, 1)
                elif piece == 4:
                    wait(act, ln_scaled, c + 1)
                    for t in range(CT):
                        m = nc.scalar.activation(conv[:, t, :], centred_sb[:, t, :], ACT.Silu,
                                                 bias=ln[:, 1, t:t + 1], scale=ln[:, 0, t:t + 1])
                    m.then_inc(silu_done, 1)
                    if overlapped:
                        prepare_heads(act, c, 4)
                        prepare_heads(act, c, 5)
                elif piece == 5:
                    wait(act, silu_done, c + 1)
                    nc.scalar.activation(in_hi[:, c & 1, 0:CT, :], conv[:, :, :], ACT.Copy).then_inc(s_hi_ready, 1)

            def product(c, t):
                b = t % 2
                wait(act, m_stored[b], c * (16 * DC) + (32 * (t // 2) + 32))
                wait(act, merged, c * DC + (t + 1))
                nc.scalar.activation(m_pair[:, b, 0, :].bitcast(F32R), prod_c[:, b, :], ACT.Copy)\
                  .then_inc(m_hi_ready, 1)

            high(0)
            for k, pieces in ((1, (1,)), (2, (2,)), (3, (4,)), (4, ()), (5, ()), (6, ()), (7, (5,))):
                high(k)
                for piece in pieces:
                    prepare(0, piece, overlapped=False)
            for piece in (4, 5):
                prepare_heads(act, 0, piece)
            over_chunks(act, prepare, product)

        @block.vector
        def _(dve):
            dve.sem_inc(s_lo_ready, 1)
            dve.sem_inc(y_taken, 4)

            def low(k):
                wait(dve, w_hi_ready, k + 1)
                nc.vector.tensor_tensor(w_lo[:, k, :], w_raw[:, k % 2, :], raw(w_hi[:, k, :]), ALU.subtract)\
                  .then_inc(w_ready, 1)

            wait(dve, param_loaded, 48)

            def over_channels(ap):
                return ap.rearrange("p (o n) -> p o n", o=1).to_broadcast([P, CT, 512])

            def prepare(c, piece, overlapped=True):
                if piece == 0:
                    wait(dve, mean_done, c + 1)
                    nc.vector.tensor_tensor(centred_sb[:, :, :], conv[:, :, :], over_channels(stat_bank[:, 0, :]),
                                            ALU.subtract).then_inc(centred, 1)
                elif piece == 2:
                    wait(dve, ln_root_ready, c + 1)
                    nc.vector.reciprocal(inv_root[:, :], root[:, :]).then_inc(ln_inv_ready, 1)
                elif piece == 3:
                    wait(dve, ln_inv_ready, c + 1)
                    nc.vector.tensor_tensor(centred_sb[:, :, :], centred_sb[:, :, :], over_channels(inv_root[:, :]),
                                            ALU.mult).then_inc(ln_scaled, 1)
                elif piece == 5:
                    wait(dve, s_hi_ready, c + 1)
                    nc.vector.tensor_tensor(in_lo[:, c & 1, 0:CT, :], conv[:, :, :],
                                            raw(in_hi[:, c & 1, 0:CT, :]), ALU.subtract).then_inc(s_lo_ready, 1)
                if overlapped:
                    for heads_piece in {1: (0, 1), 2: (2,), 3: (3,)}.get(piece, ()):
                        prepare_heads(dve, c, heads_piece)

            def product(c, t):
                b = t % 2
                wait(dve, gates_loaded[b], c * (16 * DC) + (32 * (t // 2) + 32))
                wait(dve, m_lo_ready, c * DC + (t + 1))
                wait(dve, y_done, c * (2 * DC) + (2 * t + 1))
                nc.vector.scalar_tensor_tensor(out=prod_c[:, b, :], in0=y_bank[:, b, 0, :],
                                               scalar=b_out[:, t:t + 1], in1=gates[:, b, 0, :],
                                               op0=ALU.add, op1=ALU.mult).then_inc(y_taken, 1)
                wait(dve, y_done, c * (2 * DC) + (2 * t + 2))
                nc.vector.tensor_tensor(prod_a[:, b, :], y_bank[:, b, 1, :], gates[:, b, 1, :], ALU.mult)\
                  .then_inc(y_taken, 1)
                wait(dve, y_taken, c * (2 * DC) + (2 * t + 6))
                nc.vector.tensor_tensor(prod_c[:, b, :], prod_c[:, b, :], prod_a[:, b, :], ALU.add)\
                  .then_inc(merged, 1)

            low(0)
            for k, piece in ((1, 0), (2, 2), (3, 3)):
                low(k)
                prepare(0, piece, overlapped=False)
            for piece in range(4):
                prepare_heads(dve, 0, piece)
            for k in range(4, W_CHUNKS):
                low(k)
            prepare(0, 5, overlapped=False)
            over_chunks(dve, prepare, product)

EMPTY = 1 << 24
MORE_JOBS = 32


def stage_route(nc, x, norm2_g, w_out, w_group, b_group, w_router, b_router,
                merged_d, h_d, hn_d, table_d, jobs_d, weight_d, first_weights):
    CHUNK = 4
    NC = NT // CHUNK
    R = GROUPS + EXPERTS
    with ExitStack() as ctx:
        def sb(name, shape, dt=F32):
            return ctx.enter_context(nc.sbuf_tensor("route_" + name, shape, dt))

        def sem(name):
            return ctx.enter_context(nc.semaphore("route_" + name))

        wait = register_waits(sem)

        w_raw = first_weights.gate_up[:, 0].rearrange("p k c n -> p (k c n)").rearrange("p (k n) -> p k n", n=D)
        w_hi = sb("wo_hi", [P, DC, D], F32R)
        w_lo = sb("wo_lo", [P, DC, D], F32R)
        r_raw = first_weights.gate_up[:, 1].rearrange("p k c n -> p (k c n)")[:, 0:DC * R]\
                                           .rearrange("p (c n) -> p c n", n=R)
        r_hi = sb("r_hi", [P, DC, R], F32R)
        r_lo = sb("r_lo", [P, DC, R], F32R)
        r_bias = sb("r_bias", [R, 1])
        gain = sb("gain2", [P, D])
        m_hi = sb("mT_hi", [P, 2, DC, P], F32R)
        m_lo = sb("mT_lo", [P, 2, DC, P], F32R)
        x_sb = sb("x_sb", [P, 2, D])
        h_sb = sb("h_sb", [P, 2, D])
        hn_sb = sb("hn_sb", [P, 2, D])
        stat = sb("stat2", [P, 2, 8])
        hnT_hi = sb("hnT_hi", [P, DC, CHUNK * P], F32R)
        hnT_lo = sb("hnT_lo", [P, DC, CHUNK * P], F32R)
        logitT = sb("logitT", [R, CHUNK * P])
        logit = sb("logit", [P, CHUNK, R])
        small = sb("small", [P, 12, CHUNK])
        eight = sb("eight", [P, 12, CHUNK, 8])
        onehot = sb("onehot", [P, 3, CHUNK, EXPERTS])
        product64 = sb("product64", [P, CHUNK, EXPERTS])
        both16 = sb("both16", [P, CHUNK, EXPERTS], BF16)
        seen = sb("seen", [P, EXPERTS])
        seen16 = sb("seen16", [P, CHUNK, EXPERTS], BF16)
        place = sb("place", [P, CHUNK, EXPERTS])
        slot_f = sb("slot_f", [P, 2, CHUNK])
        slot = sb("slot", [P, 2, CHUNK], I32)
        entry_now = sb("entry_now", [P, 2, CHUNK], I32)
        entry = sb("entry", [P, 2, NT], I32)
        weight = sb("weight", [P, 2, NT])
        starts = sb("starts", [EXPERTS, NT - 1])
        exists = sb("exists", [EXPERTS, NT - 1])
        extra = sb("extra", [EXPERTS, 1])
        extra16 = sb("extra16", [EXPERTS, MORE_JOBS], BF16)
        lane = sb("lane", [MORE_JOBS, 1])
        ended = sb("ended", [MORE_JOBS, 2, EXPERTS])
        job_f = sb("job_f", [MORE_JOBS, 4])
        job = sb("job", [MORE_JOBS, 2], I32)
        job_count = sb("job_count", [1, 1], I32)
        ident = sb("ident", [P, P])
        earlier = sb("earlier", [P, P], BF16)
        ones16 = sb("ones16", [P, P], BF16)
        index8 = sb("index8", [P, 8])
        index64 = sb("index64", [P, EXPERTS])
        index64_tiled = sb("index64_tiled", [P, CHUNK * EXPERTS])
        empty = first_weights.down[:, 0, 0, 0:SEQ * EXPERTS // P].bitcast(I32)
        h_bank = ctx.enter_context(nc.psum_tensor("route_h_bank", [P, 2, 2, 512], F32))
        t_bank = ctx.enter_context(nc.psum_tensor("route_t_bank", [P, 2, 512], F32))
        r_bank = ctx.enter_context(nc.psum_tensor("route_r_bank", [P, 512], F32))
        s_bank = ctx.enter_context(nc.psum_tensor("route_s_bank", [P, 512], F32))

        consts_ready = sem("consts_ready")
        param_loaded = sem("param_loaded")
        table_cleared = sem("table_cleared")
        w_loaded = [sem(f"w_loaded{i}") for i in range(4)]
        r_loaded = sem("r_loaded")
        w_hi_ready = sem("w_hi_ready")
        w_ready = sem("w_ready")
        in_loaded = [sem("in_loaded0"), sem("in_loaded1")]
        h_done = sem("h_done")
        h_ready = sem("h_ready")
        squares_summed = sem("squares_summed")
        var_ready = sem("var_ready")
        root_ready = sem("root_ready")
        newton_step = sem("newton_step")
        hn_ready = sem("hn_ready")
        hn_turned = sem("hn_turned")
        hn_hi_ready = sem("hn_hi_ready")
        hn_lo_ready = sem("hn_lo_ready")
        stored = [sem("stored0"), sem("stored1")]
        logits_done = sem("logits_done")
        logitT_ready = sem("logitT_ready")
        logits_turned = sem("logits_turned")
        choice_step = sem("choice_step")
        exp_ready = sem("exp_ready")
        both_ready = sem("both_ready")
        rank_done = sem("rank_done")
        slots_ready = sem("slots_ready")
        slots_free = sem("slots_free")
        scattered = sem("scattered")
        counts_done = sem("counts_done")
        seen_step = sem("seen_step")
        weight_step = sem("weight_step")
        slot_step = sem("slot_step")
        tiled = sem("tiled")
        final_step = sem("final_step")
        final_stored = sem("final_stored")

        STEPS, EXP_STEP = 32, 21

        block = ctx.enter_context(nc.Block())
        x_tiles = x.rearrange("(t p) d -> t p d", p=P)
        h_tiles = h_d.rearrange("(t p) d -> t p d", p=P)
        hn_tiles = hn_d.rearrange("(t p) d -> t p d", p=P)

        def over_chunks(eng, tile, tail, after):
            for j in range(CHUNK):
                tile(0, j)
                if j:
                    after(0, j - 1)
            with eng.Fori(1, NC) as c:
                for j in range(CHUNK):
                    tile(c, j)
                    tail(c - 1, j, False)
                    if j:
                        after(c, j - 1)
                    tail(c - 1, j, True)
            for j in range(CHUNK):
                tail(NC - 1, j, False)
                tail(NC - 1, j, True)

        @block.sync
        def _(sp):
            def load_tile(n, b):
                wait(sp, h_ready, n + 1)
                sp.dma_start(raw(m_hi[:, b, :, :]), merged_d[n, :, :, 0, :]).then_inc(in_loaded[b], 16)
                sp.dma_start(raw(m_lo[:, b, :, :]), merged_d[n, :, :, 1, :]).then_inc(in_loaded[b], 16)
                sp.dma_start(x_sb[:, b, :], x_tiles[n]).then_inc(in_loaded[b], 16)

            for k in range(DC):
                if k == 2:
                    load_tile(0, 0)
                if k >= 4:
                    wait(sp, w_ready, k - 3)
                sp.dma_start(w_raw[:, k % 4, :], w_out[k * P:(k + 1) * P, :]).then_inc(w_loaded[k % 4], 16)
            sp.dma_start(r_raw[:, :, 0:GROUPS], w_group.rearrange("(c p) n -> p c n", p=P)).then_inc(r_loaded, 16)
            sp.dma_start(r_raw[:, :, GROUPS:R], w_router.rearrange("(c p) n -> p c n", p=P)).then_inc(r_loaded, 16)
            sp.dma_start(r_bias[0:GROUPS, :], b_group.rearrange("(p o) -> p o", o=1),
                         allow_slow_non_contiguous=True).then_inc(param_loaded, 16)
            sp.dma_start(r_bias[GROUPS:R, :], b_router.rearrange("(p o) -> p o", o=1),
                         allow_slow_non_contiguous=True).then_inc(param_loaded, 16)
            sp.dma_start(gain[:, :], norm2_g.rearrange("(o d) -> o d", o=1).to_broadcast([P, D]))\
              .then_inc(param_loaded, 16)
            load_tile(1, 1)
            wait(sp, consts_ready, 11)
            sp.dma_start(table_d.rearrange("(p n) o -> p (n o)", p=P), empty).then_inc(table_cleared, 16)
            with sp.Fori(1, NT // 2) as it:
                for b in range(2):
                    load_tile(it * 2 + b, b)
            wait(sp, w_ready, DC + 1)
            wait(sp, table_cleared, 16)
            for e in range(2):
                first_weights.load(sp, e, e)
            for s in stored:
                wait(sp, s, 32 + 16 * NT)

        @block.gpsimd
        def _(pool):
            def chain(m, n):
                m.then_inc(consts_ready, 1)
                wait(pool, consts_ready, n)

            chain(nc.gpsimd.memset(ident[:, :], 0.0), 1)
            chain(nc.gpsimd.affine_select(out=ident[:, :], in_=ident[:, :], compare_op=ALU.not_equal, fill=1.0,
                                          base=0, pattern=[[-1, P]], channel_multiplier=1), 2)
            chain(nc.gpsimd.memset(ones16[:, :], 1.0), 3)
            chain(nc.gpsimd.affine_select(out=earlier[:, :], in_=ones16[:, :], compare_op=ALU.is_gt, fill=0.0,
                                          base=0, pattern=[[1, P]], channel_multiplier=-1), 4)
            chain(nc.gpsimd.iota(index8[:, :], [[1, 8]], base=-8, channel_multiplier=0,
                                 allow_small_or_imprecise_dtypes=True), 5)
            chain(nc.gpsimd.iota(index64[:, :], [[1, EXPERTS]], base=0, channel_multiplier=0,
                                 allow_small_or_imprecise_dtypes=True), 6)
            chain(nc.gpsimd.iota(entry[:, :, :], [[1, 2], [2 * P, NT]], base=0, channel_multiplier=2), 7)
            chain(nc.gpsimd.memset(seen[:, :], 0.0), 8)
            chain(nc.gpsimd.memset(empty, EMPTY), 9)
            chain(nc.gpsimd.iota(starts[:, :], [[P, NT - 1]], base=P, channel_multiplier=0,
                                 allow_small_or_imprecise_dtypes=True), 10)
            chain(nc.gpsimd.iota(lane[:, :], [[1, 1]], base=0, channel_multiplier=1,
                                 allow_small_or_imprecise_dtypes=True), 11)
            wait(pool, table_cleared, 16)
            pool.sem_inc(slots_free, 1)

            def scatter(c):
                wait(pool, slots_ready, c * 3 + 3)
                for j in range(CHUNK):
                    for k in range(2):
                        pool.indirect_dma_start(
                            out=table_d, out_offset=bass.IndirectOffsetOnAxis(
                                ap=slot[:, k, j:j + 1], axis=0),
                            in_=entry_now[:, k, j:j + 1], in_offset=None).then_inc(scattered, 16)
                wait(pool, scattered, c * (32 * CHUNK) + 32 * CHUNK)
                pool.sem_inc(slots_free, 1)

            with pool.Fori(0, NC) as c:
                scatter(c)

        @block.tensor
        def _(pe):
            pe.wait_ge(consts_ready, 11)

            def turn(c, j):
                n = c * CHUNK + j
                pe.wait_ge(hn_ready, n + 1)
                pe.wait_ge(hn_lo_ready, n + 1)
                for i in range(DC):
                    m = nc.tensor.transpose(t_bank[:, i // 4, (i % 4) * P:(i % 4 + 1) * P],
                                            hn_sb[:, j % 2, i * P:(i + 1) * P], ident[:, :])
                m.then_inc(hn_turned, 1)

            def tile(c, j):
                n = c * CHUNK + j
                b = j % 2
                first = isinstance(c, int) and j == 0
                pe.wait_ge(in_loaded[b], c * 96 + (48 * (j // 2) + 48))
                pe.wait_ge(h_ready, n + 1)
                for half in range(2):
                    cols = slice(512 * half, 512 * (half + 1))
                    for i in range(DC):
                        if first and half == 0:
                            pe.wait_ge(w_ready, i + 1)
                        m = pair_matmuls(nc.tensor, h_bank[:, b, half, :], (m_hi[:, b, i, :], m_lo[:, b, i, :]),
                                         (w_hi[:, i, cols], w_lo[:, i, cols]), i == 0, i == DC - 1)
                m.then_inc(h_done, 1)

            def tail(c, part, behind):
                if part == 0 and not behind:
                    turn(c, CHUNK - 1)
                elif part == 1 and not behind:
                    pe.wait_ge(hn_lo_ready, c * CHUNK + (CHUNK + 1))
                    pe.wait_ge(w_ready, DC + 1)
                    for i in range(DC):
                        m = pair_matmuls(nc.tensor, r_bank[0:R, :], (r_hi[:, i, :], r_lo[:, i, :]),
                                         (hnT_hi[:, i, :], hnT_lo[:, i, :]), i == 0, i == DC - 1)
                    m.then_inc(logits_done, 1)
                elif part == 1:
                    pe.wait_ge(logitT_ready, c + 1)
                    for j in range(CHUNK):
                        m = nc.tensor.transpose(s_bank[:, j * R:(j + 1) * R], logitT[:, j * P:(j + 1) * P],
                                                ident[0:R, 0:R])
                    m.then_inc(logits_turned, 1)
                elif part == 3 and behind:
                    pe.wait_ge(both_ready, c + 1)
                    for j in range(CHUNK):
                        out = r_bank[:, j * EXPERTS:(j + 1) * EXPERTS]
                        nc.tensor.matmul(out, earlier[:, :], both16[:, j, :], start=True, stop=False)
                        m = nc.tensor.matmul(out, ones16[:, :], seen16[:, j, :], start=False, stop=True)
                    m.then_inc(rank_done, 1)

            over_chunks(pe, tile, tail, turn)
            pe.wait_ge(final_step, 1)
            nc.tensor.matmul(s_bank[0:EXPERTS, 0:1], both16[:, 0, :], ones16[:, 0:1], start=True, stop=True)\
              .then_inc(counts_done, 1)
            pe.wait_ge(final_step, 4)
            nc.tensor.matmul(r_bank[0:MORE_JOBS, 0:EXPERTS], extra16[:, :], earlier[0:EXPERTS, 1:EXPERTS + 1],
                             start=True, stop=True).then_inc(counts_done, 1)

        @block.scalar
        def _(act):
            for s in stored:
                act.sem_inc(s, 32)
            for k in range(DC):
                wait(act, w_loaded[k % 4], 16 * (k // 4 + 1))
                nc.scalar.activation(w_hi[:, k, :], w_raw[:, k % 4, :], ACT.Copy).then_inc(w_hi_ready, 1)
            wait(act, r_loaded, 32)
            nc.scalar.activation(r_hi[:, :, :], r_raw[:, :, :], ACT.Copy).then_inc(w_hi_ready, 1)
            wait(act, param_loaded, 48)

            def high(c, j):
                n = c * CHUNK + j
                wait(act, hn_turned, n + 1)
                nc.scalar.activation(hnT_hi[:, :, j * P:(j + 1) * P],
                                     t_bank[:, :, :].rearrange("p b (c t) -> p (b c) t", t=P), ACT.Copy)\
                  .then_inc(hn_hi_ready, 1)

            def tile(c, j):
                n = c * CHUNK + j
                b = j % 2
                wait(act, h_ready, n + 3)
                nc.scalar.activation(hn_sb[:, b, :], h_sb[:, b, :], ACT.Square, accum_out=stat[:, b, 0:1])\
                  .then_inc(squares_summed, 1)
                wait(act, var_ready, n + 1)
                nc.scalar.activation(stat[:, b, 2:3], stat[:, b, 1:2], ACT.Sqrt).then_inc(root_ready, 1)
                wait(act, hn_ready, n + 1)
                act.dma_start(h_tiles[n], h_sb[:, b, :]).then_inc(stored[b], 16)
                act.dma_start(hn_tiles[n], hn_sb[:, b, :]).then_inc(stored[b], 16)

            def tail(c, part, behind):
                if part == 0 and not behind:
                    high(c, CHUNK - 1)
                elif part == 1 and not behind:
                    wait(act, logits_done, c + 1)
                    nc.scalar.activation(logitT[:, :], r_bank[0:R, :], ACT.Identity, bias=r_bias[:, 0:1])\
                      .then_inc(logitT_ready, 1)
                elif part == 1:
                    wait(act, choice_step, c * STEPS + EXP_STEP)
                    nc.scalar.activation(eight[:, 8, :, :], eight[:, 0, :, :], ACT.Exp).then_inc(exp_ready, 1)
                    nc.scalar.activation(small[:, 6, :], small[:, 5, :], ACT.Exp).then_inc(exp_ready, 1)

            over_chunks(act, tile, tail, high)
            wait(act, final_step, 13)
            act.dma_start(jobs_d[:, 0:1], job_count[:, :]).then_inc(final_stored, 16)
            for k in range(2):
                act.dma_start(jobs_d[:, 1 + MORE_JOBS * k:1 + MORE_JOBS * (k + 1)].rearrange("o j -> j o"),
                              job[:, k:k + 1], allow_slow_non_contiguous=True).then_inc(final_stored, 16)
            wait(act, weight_step, 2 * NC)
            act.dma_start(weight_d, weight[:, :, :].rearrange("p k t -> p (k t)")).then_inc(final_stored, 16)
            wait(act, final_stored, 64)

        @block.vector
        def _(dve):
            dve.sem_inc(h_ready, 2)
            dve.sem_inc(hn_lo_ready, 1)
            for k in range(DC):
                wait(dve, w_hi_ready, k + 1)
                nc.vector.tensor_tensor(w_lo[:, k, :], w_raw[:, k % 4, :], raw(w_hi[:, k, :]), ALU.subtract)\
                  .then_inc(w_ready, 1)
            wait(dve, w_hi_ready, DC + 1)
            nc.vector.tensor_tensor(r_lo[:, :, :], r_raw[:, :, :], raw(r_hi[:, :, :]), ALU.subtract)\
              .then_inc(w_ready, 1)
            wait(dve, param_loaded, 48)
            wait(dve, consts_ready, 11)

            def lower(c, j):
                n = c * CHUNK + j
                wait(dve, hn_hi_ready, n + 1)
                nc.vector.tensor_tensor(hnT_lo[:, :, j * P:(j + 1) * P],
                                        t_bank[:, :, :].rearrange("p b (c t) -> p (b c) t", t=P),
                                        raw(hnT_hi[:, :, j * P:(j + 1) * P]), ALU.subtract).then_inc(hn_lo_ready, 1)

            def tile(c, j):
                n = c * CHUNK + j
                b = j % 2
                s = stat[:, b, :]
                wait(dve, in_loaded[b], c * 96 + (48 * (j // 2) + 48))
                wait(dve, stored[b], c * 64 + (32 * (j // 2) + 32))
                wait(dve, h_done, n + 1)
                nc.vector.tensor_tensor(h_sb[:, b, :], h_bank[:, b, :, :].rearrange("p k n -> p (k n)"),
                                        x_sb[:, b, :], ALU.add).then_inc(h_ready, 1)
                wait(dve, squares_summed, n + 1)
                nc.vector.tensor_scalar(s[:, 1:2], s[:, 0:1], 1.0 / D, RMS_EPS, ALU.mult, ALU.add)\
                  .then_inc(var_ready, 1)
                wait(dve, root_ready, n + 1)
                nc.vector.reciprocal(s[:, 3:4], s[:, 2:3]).then_inc(newton_step, 1)
                wait(dve, newton_step, n * 4 + 1)
                nc.vector.scalar_tensor_tensor(out=s[:, 4:5], in0=s[:, 3:4], scalar=s[:, 1:2], in1=s[:, 3:4],
                                               op0=ALU.mult, op1=ALU.mult).then_inc(newton_step, 1)
                wait(dve, newton_step, n * 4 + 2)
                nc.vector.tensor_scalar(s[:, 5:6], s[:, 4:5], -0.5, 1.5, ALU.mult, ALU.add)\
                  .then_inc(newton_step, 1)
                wait(dve, newton_step, n * 4 + 3)
                nc.vector.tensor_tensor(s[:, 6:7], s[:, 5:6], s[:, 3:4], ALU.mult).then_inc(newton_step, 1)
                wait(dve, newton_step, n * 4 + 4)
                nc.vector.scalar_tensor_tensor(out=hn_sb[:, b, :], in0=h_sb[:, b, :], scalar=s[:, 6:7],
                                               in1=gain[:, :], op0=ALU.mult, op1=ALU.mult).then_inc(hn_ready, 1)

            def wide(ap, n=8):
                return ap.rearrange("p (t o) -> p t o", o=1).to_broadcast([P, CHUNK, n])

            def each_tile(ap):
                return ap.rearrange("p (o n) -> p o n", o=1).to_broadcast([P, CHUNK, ap.shape[-1]])

            def choose(c):
                count = [0]

                def step(m):
                    count[0] += 1
                    m.then_inc(choice_step, 1)
                    wait(dve, choice_step, c * STEPS + count[0])

                v = nc.vector
                s = lambda i: small[:, i, :]
                e = lambda i: eight[:, i, :, :]

                def first_max(values, top, mark):
                    step(v.tensor_reduce(top, values, AX.X, ALU.max))
                    step(v.tensor_tensor(e(9), values, wide(top), ALU.is_equal))
                    step(v.tensor_tensor(e(10), e(9), each_tile(index8[:, :]), ALU.mult))
                    step(v.tensor_reduce(s(9), e(10), AX.X, ALU.min))
                    step(v.tensor_tensor(mark, each_tile(index8[:, :]), wide(s(9)), ALU.is_equal))

                wait(dve, logits_turned, c + 1)
                step(v.tensor_copy(logit[:, :, :], s_bank[:, 0:CHUNK * R].rearrange("p (t n) -> p t n", n=R)))
                groups = logit[:, :, 0:GROUPS]
                experts = logit[:, :, GROUPS:R].rearrange("p t (g j) -> p t g j", j=PER_GROUP)
                first_max(groups, s(0), e(1))
                step(v.tensor_tensor(e(0), groups, wide(s(0)), ALU.subtract))
                p64 = product64[:, :, :]
                step(v.tensor_tensor(p64.rearrange("p t (g j) -> p t g j", j=PER_GROUP), experts,
                                     e(1).rearrange("p t (g o) -> p t g o", o=1)
                                         .to_broadcast([P, CHUNK, GROUPS, PER_GROUP]), ALU.mult))
                step(v.tensor_reduce(e(2), p64.rearrange("p t (g j) -> p t j g", j=PER_GROUP), AX.X, ALU.add))
                first_max(e(2), s(1), e(3))
                step(v.scalar_tensor_tensor(out=e(4), in0=e(3), scalar=-3e38, in1=e(2),
                                            op0=ALU.mult, op1=ALU.add))
                first_max(e(4), s(2), e(5))
                step(v.tensor_tensor(s(5), s(2), s(1), ALU.subtract))
                for k in range(2):
                    mark = onehot[:, k, :, :].rearrange("p t (g j) -> p t g j", j=PER_GROUP)
                    inner = e(3 + 2 * k).rearrange("p t (o j) -> p t o j", o=1)\
                                        .to_broadcast([P, CHUNK, GROUPS, PER_GROUP])
                    outer = e(1).rearrange("p t (g o) -> p t g o", o=1)\
                                .to_broadcast([P, CHUNK, GROUPS, PER_GROUP])
                    step(v.tensor_tensor(mark, inner, outer, ALU.mult))
                step(v.tensor_tensor(onehot[:, 2, :, :], onehot[:, 0, :, :], onehot[:, 1, :, :], ALU.add))
                for j in range(CHUNK):
                    step(v.tensor_copy(seen16[:, j, :], seen[:, :]))
                    v.tensor_tensor(seen[:, :], seen[:, :], onehot[:, 2, j, :], ALU.add).then_inc(seen_step, 1)
                    wait(dve, seen_step, c * CHUNK + (j + 1))
                v.tensor_copy(both16[:, :, :], onehot[:, 2, :, :]).then_inc(both_ready, 1)
                wait(dve, exp_ready, c * 2 + 2)
                step(v.tensor_reduce(s(3), e(8), AX.X, ALU.add))
                step(v.tensor_scalar(s(4), s(6), 1.0, None, ALU.add))
                step(v.tensor_tensor(s(7), s(3), s(4), ALU.mult))
                step(v.reciprocal(s(8), s(7)))
                cols = bass.ds(c * CHUNK, CHUNK)
                v.tensor_copy(weight[:, 0, cols], s(8)).then_inc(weight_step, 1)
                v.tensor_tensor(weight[:, 1, cols], s(8), s(6), ALU.mult).then_inc(weight_step, 1)
                assert count[0] == STEPS, count[0]

            def find_slots(c):
                v = nc.vector
                wait(dve, rank_done, c + 1)
                v.scalar_tensor_tensor(out=place[:, :, :].rearrange("p t n -> p (t n)"),
                                       in0=r_bank[:, 0:CHUNK * EXPERTS], scalar=float(EXPERTS),
                                       in1=index64_tiled[:, :], op0=ALU.mult, op1=ALU.add).then_inc(slot_step, 1)
                wait(dve, slot_step, c * 5 + 1)
                wait(dve, slots_free, c + 1)
                v.tensor_copy(entry_now[:, :, :], entry[:, :, bass.ds(c * CHUNK, CHUNK)]).then_inc(slots_ready, 1)
                for k in range(2):
                    v.tensor_tensor(product64[:, :, :], place[:, :, :], onehot[:, k, :, :], ALU.mult)\
                     .then_inc(slot_step, 1)
                    wait(dve, slot_step, c * 5 + (2 * k + 2))
                    v.tensor_reduce(slot_f[:, k, :], product64[:, :, :], AX.X, ALU.add).then_inc(slot_step, 1)
                    wait(dve, slot_step, c * 5 + (2 * k + 3))
                    v.tensor_copy(slot[:, k, :], slot_f[:, k, :]).then_inc(slots_ready, 1)

            def tail(c, part, behind):
                if part == 0 and not behind:
                    lower(c, CHUNK - 1)
                elif part == 1 and behind:
                    choose(c)
                elif part == 3 and behind:
                    find_slots(c)

            for j in range(CHUNK):
                nc.vector.tensor_copy(index64_tiled[:, j * EXPERTS:(j + 1) * EXPERTS], index64[:, :])\
                  .then_inc(tiled, 1)
            wait(dve, tiled, CHUNK)
            over_chunks(dve, tile, tail, lower)

            v = nc.vector

            def final(m, n):
                m.then_inc(final_step, 1)
                wait(dve, final_step, n)

            wait(dve, seen_step, NT)
            final(v.tensor_copy(both16[:, 0, :], seen[:, :]), 1)
            wait(dve, counts_done, 1)
            final(v.tensor_tensor(exists[:, :], starts[:, :],
                                  s_bank[0:EXPERTS, 0:1].to_broadcast([EXPERTS, NT - 1]), ALU.is_lt), 2)
            final(v.tensor_reduce(extra[:, :], exists[:, :], AX.X, ALU.add), 3)
            final(v.tensor_copy(extra16[:, :], extra[:, :].to_broadcast([EXPERTS, MORE_JOBS])), 4)
            wait(dve, counts_done, 2)
            upto = r_bank[0:MORE_JOBS, 0:EXPERTS]
            final(v.tensor_tensor(ended[:, 0, :], upto, lane[:, :].to_broadcast([MORE_JOBS, EXPERTS]), ALU.is_le), 5)
            final(v.tensor_tensor(ended[:, 1, :], upto, ended[:, 0, :], ALU.mult), 6)
            final(v.tensor_reduce(job_f[:, 0:1], ended[:, 0, :], AX.X, ALU.add), 7)
            final(v.tensor_reduce(job_f[:, 1:2], ended[:, 1, :], AX.X, ALU.max), 8)
            final(v.tensor_tensor(job_f[:, 2:3], lane[:, :], job_f[:, 1:2], ALU.subtract), 9)
            final(v.tensor_scalar(job_f[:, 3:4], job_f[:, 2:3], float(P), float(P), ALU.mult, ALU.add), 10)
            v.tensor_copy(job[:, 0:1], job_f[:, 0:1]).then_inc(final_step, 1)
            v.tensor_copy(job[:, 1:2], job_f[:, 3:4]).then_inc(final_step, 1)
            v.tensor_copy(job_count[:, :], r_bank[0:1, EXPERTS - 1:EXPERTS]).then_inc(final_step, 1)


class ExpertWeights:

    def __init__(self, ctx, nc, w_gate, w_up, w_down):
        self.sources = w_gate, w_up, w_down
        self.gate_up = ctx.enter_context(nc.sbuf_tensor("weights_gate_up", [P, 2, 2, DC, DE], F32))
        self.down = ctx.enter_context(nc.sbuf_tensor("weights_down", [P, 2, DE // P, D], F32))
        self.gate_up_loaded = [ctx.enter_context(nc.semaphore(f"weights_gate_up_loaded{b}")) for b in range(2)]
        self.down_loaded = [ctx.enter_context(nc.semaphore(f"weights_down_loaded{b}")) for b in range(2)]

    def load(self, eng, b, e, between=None):
        gate, up, down = self.sources
        for k, w in enumerate((gate, up)):
            eng.dma_start(self.gate_up[:, b, k, :, :], w[e].rearrange("(p c) n -> p c n", c=DC))\
               .then_inc(self.gate_up_loaded[b], 16)
        if between:
            between()
        eng.dma_start(self.down[:, b, :, :], down[e].rearrange("(p c) n -> p c n", c=DE // P))\
           .then_inc(self.down_loaded[b], 16)


def stage_experts(nc, weights, hn_d, table_d, jobs_d, y_d):
    HC = DE // P
    KH = DC // 2
    LISTS = 8
    with ExitStack() as ctx:
        def sb(name, shape, dt=F32):
            return ctx.enter_context(nc.sbuf_tensor("experts_" + name, shape, dt))

        def sem(name):
            return ctx.enter_context(nc.semaphore("experts_" + name))

        wait = register_waits(sem)

        gu_raw = weights.gate_up
        gu_hi = sb("gu_hi", [P, 2, 2, DC, DE], F32R)
        gu_lo = sb("gu_lo", [P, 2, 2, DC, DE], F32R)
        down_raw = weights.down
        down_hi = sb("down_hi", [P, 2, HC, D], F32R)
        down_lo = sb("down_lo", [P, 2, HC, D], F32R)
        rows = sb("rows", [P, 2, D])
        xT_hi = sb("xT_hi", [P, 2, DC, P], F32R)
        xT_lo = sb("xT_lo", [P, 2, DC, P], F32R)
        silu = sb("silu", [P, DE])
        hidden = sb("hidden", [P, 2, DE])
        hT_hi = sb("hT_hi", [P, 2, HC, P], F32R)
        hT_lo = sb("hT_lo", [P, 2, HC, P], F32R)
        y_sb = sb("y_sb", [P, 2, D])
        table = sb("table", [P, EXPERTS], I32)
        columns = sb("columns", [P, MORE_JOBS + 1], I32)
        job_sb = sb("job_sb", [1, 2 + 2 * MORE_JOBS], I32)
        from_row = sb("from_row", [P, 2], I32)
        to_row = sb("to_row", [P, 2], I32)
        ident = sb("ident_e", [P, P])
        gu_bank = ctx.enter_context(nc.psum_tensor("experts_gu_bank", [P, 2, 512], F32))
        x_bank = ctx.enter_context(nc.psum_tensor("experts_x_bank", [P, 2, 512], F32))
        y_bank = ctx.enter_context(nc.psum_tensor("experts_y_bank", [P, 2, 2, 512], F32))

        consts_ready = sem("consts_ready_e")
        table_loaded = sem("table_loaded")
        jobs_loaded = sem("jobs_loaded")
        gu_loaded = weights.gate_up_loaded
        down_loaded = weights.down_loaded
        columns_loaded = sem("columns_loaded")
        rows_loaded = [sem("rows_loaded0"), sem("rows_loaded1")]
        index_ready = sem("index_ready")
        x_turned = sem("x_turned")
        x_hi_ready = sem("x_hi_ready")
        x_lo_ready = sem("x_lo_ready")
        gu_hi_ready = sem("gu_hi_ready")
        gu_lo_ready = sem("gu_lo_ready")
        gu_done = sem("gu_done")
        silu_ready = sem("silu_ready")
        hidden_ready = sem("hidden_ready")
        hidden_turned = sem("hidden_turned")
        h_hi_ready = sem("h_hi_ready")
        h_lo_ready = sem("h_lo_ready")
        down_hi_ready = sem("down_hi_ready")
        down_lo_ready = sem("down_lo_ready")
        down_done = sem("down_done")
        y_ready = sem("y_ready")
        y_scattered = [sem("y_scattered0"), sem("y_scattered1")]
        y_free = sem("y_free")
        pair_passed = {name: sem(f"pair_passed_{name}") for name in ("SP", "Pool", "PE", "Activation", "DVE")}

        block = ctx.enter_context(nc.Block())
        table_rows = table_d.rearrange("(r e) o -> r (e o)", e=EXPERTS)

        def over_first_jobs(eng, step):
            for n in range(4):
                step(n, n % 2, n // 2, min(n, 3), 2)
            with eng.Fori(2, EXPERTS // 2 - 1) as q:
                for b in range(2):
                    step(q * 2 + b, b, q, 3, 2)
            step(EXPERTS - 2, 0, EXPERTS // 2 - 1, 3, 1)

        def over_further_jobs(eng, parts):
            wait(eng, jobs_loaded, 16)
            count = eng.value_load(job_sb[0:1, 0:1], min_val=0, max_val=MORE_JOBS)
            if eng is nc.vector:
                with eng.If(count > 0):
                    wait(eng, columns_loaded, count * 16)
            for ahead, part in parts:
                if ahead:
                    with eng.If(count > 0):
                        part(EXPERTS, 0, EXPERTS // 2)
                elif part:
                    part(EXPERTS - 1, 1, EXPERTS // 2 - 1)
            key = str(eng.engine).split(".")[-1]
            with eng.Fori(0, MORE_JOBS // LISTS) as many:
                with eng.If(many * LISTS < count):
                    with eng.Fori(0, LISTS // 2) as few:
                        i = many * (LISTS // 2) + few
                        with eng.If(i * 2 < count):
                            for b in range(2):
                                for ahead, part in parts:
                                    if ahead:
                                        with eng.If(i * 2 + (b + 1) < count):
                                            part(i * 2 + (EXPERTS + b + 1), 1 - b, i + (EXPERTS // 2 + b))
                                    elif part:
                                        with eng.If(i * 2 + b < count):
                                            part(i * 2 + (EXPERTS + b), b, i + EXPERTS // 2)
                            eng.sem_inc(pair_passed[key], 1)
                    eng.sem_inc(pair_passed[key], 1)
            return count

        @block.sync
        def _(sp):
            sp.dma_start(table[:, :], table_rows[0:P, :]).then_inc(table_loaded, 16)
            sp.dma_start(job_sb[:, 0:1 + 2 * MORE_JOBS], jobs_d).then_inc(jobs_loaded, 16)

            def load_weights(n, b, e):
                wait(sp, gu_lo_ready, n * 2 + 2)
                weights.load(sp, b, e, between=lambda: wait(sp, down_lo_ready, n + 1))

            for n in (2, 3):
                load_weights(n, n % 2, n)
            wait(sp, jobs_loaded, 16)
            count = sp.value_load(job_sb[0:1, 0:1], min_val=0, max_val=MORE_JOBS)

            def load_list(j):
                e = sp.value_load(job_sb[0:1, bass.ds(j + 1, 1)], min_val=0, max_val=EXPERTS - 1)
                first = sp.value_load(job_sb[0:1, bass.ds(j + (1 + MORE_JOBS), 1)], min_val=0, max_val=SEQ - P)
                sp.dma_start(columns[:, bass.ds(j, 1)], table_rows[bass.ds(first, P), bass.ds(e, 1)],
                             allow_slow_non_contiguous=True).then_inc(columns_loaded, 16)

            with sp.Fori(0, MORE_JOBS // LISTS) as i:
                with sp.If(i * LISTS < count):
                    for k in range(LISTS):
                        with sp.If(i * LISTS + k < count):
                            load_list(i * LISTS + k)
                    sp.sem_inc(pair_passed["SP"], 1)
            with sp.Fori(2, EXPERTS // 2) as q:
                for b in range(2):
                    load_weights(q * 2 + b, b, q * 2 + b)

            def further(n, b, q):
                j = n - EXPERTS + 1
                e = sp.value_load(job_sb[0:1, j:j + 1] if isinstance(j, int) else job_sb[0:1, bass.ds(j, 1)],
                                  min_val=0, max_val=EXPERTS - 1)
                load_weights(n, b, e)

            over_further_jobs(sp, [(True, further)])

        @block.gpsimd
        def _(pool):
            def chain(m, n):
                m.then_inc(consts_ready, 1)
                wait(pool, consts_ready, n)

            chain(nc.gpsimd.memset(ident[:, :], 0.0), 1)
            chain(nc.gpsimd.affine_select(out=ident[:, :], in_=ident[:, :], compare_op=ALU.not_equal, fill=1.0,
                                          base=0, pattern=[[-1, P]], channel_multiplier=1), 2)
            chain(nc.gpsimd.memset(rows[:, :, :], 0.0), 3)
            pool.sem_inc(y_free, 2)
            pool.sem_inc(down_lo_ready, 2)

            def gather(n, b):
                wait(pool, index_ready, n + 1)
                wait(pool, x_turned, n + 1)
                pool.indirect_dma_start(
                    out=rows[:, b, :], out_offset=None, in_=hn_d,
                    in_offset=bass.IndirectOffsetOnAxis(ap=from_row[:, b:b + 1], axis=0),
                    bounds_check=SEQ - 1, oob_is_err=False).then_inc(rows_loaded[b], 16)

            def lower_down(n, b):
                wait(pool, down_hi_ready, n + 1)
                nc.gpsimd.tensor_tensor(down_lo[:, b, :, :], down_raw[:, b, :, :], raw(down_hi[:, b, :, :]),
                                        ALU.subtract).then_inc(down_lo_ready, 1)

            def scatter(n, b):
                wait(pool, y_ready, n + 3)
                pool.indirect_dma_start(
                    out=y_d, out_offset=bass.IndirectOffsetOnAxis(ap=to_row[:, b:b + 1], axis=0),
                    in_=y_sb[:, b, :], in_offset=None,
                    bounds_check=2 * SEQ - 1, oob_is_err=False).then_inc(y_scattered[b], 16)

            def scattered(b, q):
                wait(pool, y_scattered[b], q * 16 + 16)
                pool.sem_inc(y_free, 1)

            def step(n, b, q, before, after):
                if before >= 2:
                    scatter(n - 2, b)
                if before >= 3:
                    scattered(1 - b, q + (b - 2))
                if after == 2:
                    gather(n + 2, b)
                lower_down(n, b)

            gather(0, 0)
            gather(1, 1)
            over_first_jobs(pool, step)
            last = EXPERTS // 2 - 1
            scatter(EXPERTS - 3, 1)
            scattered(0, last - 1)
            lower_down(EXPERTS - 1, 1)
            scatter(EXPERTS - 2, 0)
            scattered(1, last - 1)
            count = over_further_jobs(pool, [
                (True, lambda n, b, q: gather(n, b)), (False, lambda n, b, q: scattered(1 - b, q + (b - 1))),
                (True, lambda n, b, q: lower_down(n, b)), (False, lambda n, b, q: scatter(n, b))])
            even = MORE_JOBS * 2 - 2
            for b in range(2):
                wait(pool, y_scattered[b], ((count + (1 - b)) & even) * 8 + 8 * EXPERTS)

        @block.tensor
        def _(pe):
            pe.sem_inc(x_turned, 2)
            pe.sem_inc(gu_done, 2)
            pe.sem_inc(down_done, 2)
            pe.sem_inc(hidden_turned, 2)
            pe.wait_ge(consts_ready, 3)

            def turn_rows(n, b, q):
                pe.wait_ge(rows_loaded[b], q * 16 + 16)
                pe.wait_ge(x_lo_ready, n + 1)
                by_chunk = rows[:, b, :].rearrange("t (p c) -> t c p", c=DC)
                for c in range(DC):
                    m = nc.tensor.transpose(x_bank[:, c // 4, (c % 4) * P:(c % 4 + 1) * P], by_chunk[:, c, :],
                                            ident[:, :])
                m.then_inc(x_turned, 1)

            def gate_up(n, b, half):
                pe.wait_ge(gu_lo_ready, n * 2 + (5 + half))
                if half == 0:
                    pe.wait_ge(x_lo_ready, n + 2)
                for c in range(KH * half, KH * (half + 1)):
                    m = pair_matmuls(nc.tensor, gu_bank[:, b, :], (xT_hi[:, b, c, :], xT_lo[:, b, c, :]),
                                     (gu_hi[:, b, :, c, :], gu_lo[:, b, :, c, :]), c == 0, c == DC - 1)
                if half:
                    m.then_inc(gu_done, 1)

            def turn_hidden(n, b):
                pe.wait_ge(hidden_ready, n + 2)
                by_chunk = hidden[:, b, :].rearrange("t (p c) -> t c p", c=HC)
                for c in range(HC):
                    m = nc.tensor.transpose(gu_bank[:, b, c * P:(c + 1) * P], by_chunk[:, c, :], ident[:, :])
                m.then_inc(hidden_turned, 1)

            def down(n, b):
                pe.wait_ge(down_lo_ready, n + 3)
                pe.wait_ge(h_lo_ready, n + 1)
                pe.wait_ge(y_ready, n + 1)
                for half in range(2):
                    cols = slice(512 * half, 512 * (half + 1))
                    for c in range(HC):
                        m = pair_matmuls(nc.tensor, y_bank[:, b, half, :], (hT_hi[:, b, c, :], hT_lo[:, b, c, :]),
                                         (down_hi[:, b, c, cols], down_lo[:, b, c, cols]), c == 0, c == HC - 1)
                m.then_inc(down_done, 1)

            def step(n, b, q, before, after):
                if after >= 1:
                    turn_rows(n + 1, 1 - b, q + b)
                gate_up(n, b, 0)
                if before >= 1:
                    turn_hidden(n - 1, 1 - b)
                gate_up(n, b, 1)
                if before >= 1:
                    down(n - 1, 1 - b)

            turn_rows(0, 0, 0)
            over_first_jobs(pe, step)
            turn_hidden(EXPERTS - 2, 0)
            down(EXPERTS - 2, 0)

            def further_products(n, b, q):
                gate_up(n, b, 0)
                gate_up(n, b, 1)

            def further_down(n, b, q):
                turn_hidden(n, b)
                down(n, b)

            over_further_jobs(pe, [(False, further_products), (True, turn_rows), (False, further_down)])

        @block.scalar
        def _(act):
            act.sem_inc(hidden_ready, 1)

            def high_gate_up(n, b, q, half):
                if half == 0:
                    wait(act, gu_loaded[b], q * 32 + 32)
                    wait(act, gu_done, n + 1)
                cut = slice(KH * half, KH * (half + 1))
                nc.scalar.activation(gu_hi[:, b, :, cut, :], gu_raw[:, b, :, cut, :], ACT.Copy)\
                  .then_inc(gu_hi_ready, 1)

            def high_down(n, b, q):
                wait(act, down_loaded[b], q * 16 + 16)
                wait(act, down_done, n + 1)
                nc.scalar.activation(down_hi[:, b, :, :], down_raw[:, b, :, :], ACT.Copy).then_inc(down_hi_ready, 1)

            def high_x(n, b):
                wait(act, x_turned, n + 3)
                wait(act, gu_done, n + 1)
                nc.scalar.activation(xT_hi[:, b, :, :], x_bank[:, :, :].rearrange("p k (c t) -> p (k c) t", t=P),
                                     ACT.Copy).then_inc(x_hi_ready, 1)

            def gate(n, b):
                wait(act, gu_done, n + 3)
                wait(act, hidden_ready, n + 1)
                nc.scalar.activation(silu[:, :], gu_bank[:, b, 0:DE], ACT.Silu).then_inc(silu_ready, 1)

            def high_hidden(n, b):
                wait(act, hidden_turned, n + 3)
                wait(act, down_done, n + 1)
                nc.scalar.activation(hT_hi[:, b, :, :], gu_bank[:, b, 0:DE].rearrange("p (c t) -> p c t", t=P),
                                     ACT.Copy).then_inc(h_hi_ready, 1)

            def step(n, b, q, before, after):
                if before >= 1:
                    gate(n - 1, 1 - b)
                if after >= 1:
                    high_x(n + 1, 1 - b)
                    high_gate_up(n + 1, 1 - b, q + b, 0)
                if before >= 1:
                    high_hidden(n - 1, 1 - b)
                if after >= 1:
                    high_gate_up(n + 1, 1 - b, q + b, 1)
                    high_down(n + 1, 1 - b, q + b)

            high_gate_up(0, 0, 0, 0)
            high_gate_up(0, 0, 0, 1)
            high_x(0, 0)
            high_down(0, 0, 0)
            over_first_jobs(act, step)
            gate(EXPERTS - 2, 0)
            high_hidden(EXPERTS - 2, 0)

            def further_weights(n, b, q):
                for half in range(2):
                    high_gate_up(n, b, q, half)

            def further_rows(n, b, q):
                high_x(n, b)
                high_down(n, b, q)

            over_further_jobs(act, [(True, further_weights), (False, lambda n, b, q: gate(n, b)),
                                    (True, further_rows), (False, lambda n, b, q: high_hidden(n, b))])

        @block.vector
        def _(dve):
            dve.sem_inc(x_lo_ready, 1)
            dve.sem_inc(gu_lo_ready, 4)
            dve.sem_inc(y_ready, 2)

            def index(n, b, entries):
                wait(dve, x_turned, n + 1)
                nc.vector.tensor_scalar(from_row[:, b:b + 1], entries, 1, None, ALU.arith_shift_right)\
                  .then_inc(index_ready, 1)

            def lower_gate_up(n, b, half):
                wait(dve, gu_hi_ready, n * 2 + (1 + half))
                cut = slice(KH * half, KH * (half + 1))
                nc.vector.tensor_tensor(gu_lo[:, b, :, cut, :], gu_raw[:, b, :, cut, :],
                                        raw(gu_hi[:, b, :, cut, :]), ALU.subtract).then_inc(gu_lo_ready, 1)

            def lower_x(n, b):
                wait(dve, x_hi_ready, n + 1)
                nc.vector.tensor_tensor(xT_lo[:, b, :, :], x_bank[:, :, :].rearrange("p k (c t) -> p (k c) t", t=P),
                                        raw(xT_hi[:, b, :, :]), ALU.subtract).then_inc(x_lo_ready, 1)

            def times_up(n, b):
                wait(dve, silu_ready, n + 1)
                wait(dve, hidden_turned, n + 1)
                nc.vector.tensor_tensor(hidden[:, b, :], silu[:, :], gu_bank[:, b, DE:2 * DE], ALU.mult)\
                  .then_inc(hidden_ready, 1)

            def lower_hidden(n, b):
                wait(dve, h_hi_ready, n + 1)
                nc.vector.tensor_tensor(hT_lo[:, b, :, :], gu_bank[:, b, 0:DE].rearrange("p (c t) -> p c t", t=P),
                                        raw(hT_hi[:, b, :, :]), ALU.subtract).then_inc(h_lo_ready, 1)

            def take_y(n, b, entries):
                wait(dve, down_done, n + 3)
                wait(dve, y_free, n + 1)
                nc.vector.tensor_copy(to_row[:, b:b + 1], entries)
                nc.vector.tensor_copy(y_sb[:, b, :], y_bank[:, b, :, :].rearrange("p k n -> p (k n)"))\
                  .then_inc(y_ready, 1)

            def list_of(n):
                return table[:, n:n + 1] if isinstance(n, int) else table[:, bass.ds(n, 1)]

            def step(n, b, q, before, after):
                if before >= 1:
                    times_up(n - 1, 1 - b)
                if before >= 2:
                    take_y(n - 2, b, list_of(n - 2))
                if after >= 2:
                    index(n + 2, b, list_of(n + 2))
                if after >= 1:
                    lower_x(n + 1, 1 - b)
                    lower_gate_up(n + 1, 1 - b, 0)
                if before >= 1:
                    lower_hidden(n - 1, 1 - b)
                if after >= 1:
                    lower_gate_up(n + 1, 1 - b, 1)

            wait(dve, table_loaded, 16)
            index(0, 0, list_of(0))
            index(1, 1, list_of(1))
            lower_gate_up(0, 0, 0)
            lower_gate_up(0, 0, 1)
            lower_x(0, 0)
            over_first_jobs(dve, step)
            times_up(EXPERTS - 2, 0)
            take_y(EXPERTS - 3, 1, list_of(EXPERTS - 3))
            lower_hidden(EXPERTS - 2, 0)
            take_y(EXPERTS - 2, 0, list_of(EXPERTS - 2))

            def further_list(n):
                j = n - EXPERTS
                return columns[:, j:j + 1] if isinstance(j, int) else columns[:, bass.ds(j, 1)]

            def further_weights(n, b, q):
                index(n, b, further_list(n))
                for half in range(2):
                    lower_gate_up(n, b, half)

            def further_products(n, b, q):
                lower_hidden(n, b)
                take_y(n, b, list_of(n) if isinstance(n, int) and n < EXPERTS else further_list(n))

            over_further_jobs(dve, [(True, further_weights), (False, lambda n, b, q: times_up(n, b)),
                                    (True, lambda n, b, q: lower_x(n, b)), (False, further_products)])


def stage_combine(nc, h_d, y_d, weight_d, out):
    BUFS = 4
    with ExitStack() as ctx:
        def sb(name, shape, dt=F32):
            return ctx.enter_context(nc.sbuf_tensor("combine_" + name, shape, dt))

        def sem(name):
            return ctx.enter_context(nc.semaphore("combine_" + name))

        wait = register_waits(sem)
        weight = sb("weight_c", [P, 2, NT])
        h_sb = sb("h_c", [P, BUFS, D])
        y_sb = sb("y_c", [P, BUFS, 2, D])
        first = sb("first_c", [P, BUFS, D])
        result = sb("result_c", [P, BUFS, D])
        weight_loaded = sem("weight_loaded")
        loaded = [sem(f"loaded_c{b}") for b in range(BUFS)]
        first_added = sem("first_added")
        added = sem("added")
        stored = [sem(f"stored_c{b}") for b in range(BUFS)]

        block = ctx.enter_context(nc.Block())
        h_tiles = h_d.rearrange("(t p) d -> t p d", p=P)
        y_tiles = y_d.rearrange("(t p k) d -> t p (k d)", p=P, k=2)
        out_tiles = out.rearrange("(t p) d -> t p d", p=P)

        @block.sync
        def _(sp):
            sp.dma_start(weight[:, :, :].rearrange("p k t -> p (k t)"), weight_d).then_inc(weight_loaded, 16)
            with sp.Fori(0, NT // BUFS) as i:
                for b in range(BUFS):
                    wait(sp, added, i * BUFS + (b + 1))
                    sp.dma_start(h_sb[:, b, :], h_tiles[i * BUFS + b]).then_inc(loaded[b], 16)
                    sp.dma_start(y_sb[:, b, :, :].rearrange("p k d -> p (k d)"), y_tiles[i * BUFS + b])\
                      .then_inc(loaded[b], 16)

        @block.vector
        def _(dve):
            dve.sem_inc(added, BUFS)
            wait(dve, weight_loaded, 16)
            with dve.Fori(0, NT // BUFS) as i:
                for b in range(BUFS):
                    t = i * BUFS + b
                    wait(dve, loaded[b], i * 32 + 32)
                    nc.vector.scalar_tensor_tensor(out=first[:, b, :], in0=y_sb[:, b, 0, :],
                                                   scalar=weight[:, 0, bass.ds(t, 1)], in1=h_sb[:, b, :],
                                                   op0=ALU.mult, op1=ALU.add).then_inc(first_added, 1)
                    wait(dve, first_added, t + 1)
                    wait(dve, stored[b], i * 16 + 16)
                    nc.vector.scalar_tensor_tensor(out=result[:, b, :], in0=y_sb[:, b, 1, :],
                                                   scalar=weight[:, 1, bass.ds(t, 1)], in1=first[:, b, :],
                                                   op0=ALU.mult, op1=ALU.add).then_inc(added, 1)

        @block.scalar
        def _(act):
            for s in stored:
                act.sem_inc(s, 16)
            with act.Fori(0, NT // BUFS) as i:
                for b in range(BUFS):
                    t = i * BUFS + b
                    wait(act, added, t + (BUFS + 1))
                    act.dma_start(out_tiles[t], result[:, b, :]).then_inc(stored[b], 16)
            for s in stored:
                wait(act, s, 16 + 16 * (NT // BUFS))


def hybrid_block(nc, x, meta, norm1_g, w_in, b_in, dw_w, dw_b, conv_ln_g, conv_ln_b, w_conv_out, b_conv_out,
                 q_norm_g, k_norm_g, b_forget, w_attn_out, w_out, norm2_g, w_group, b_group, w_router,
                 b_router, w_gate, w_up, w_down, out):
    def scratch(name, shape, dt=F32):
        return nc.dram_tensor(name, shape, dt)[:]

    conv_d = scratch("conv_d", [CT, P, SEQ])
    gate_d = scratch("gate_d", [2 * DC, P, SEQ])
    qk_d = scratch("qk_d", [2 * PAIRS, 2, P, L])
    v_d = scratch("v_d", [PAIRS, P, KT * 2 * P])
    decay_d = scratch("decay_d", [HEADS, L])
    o_d = scratch("o_d", [2 * PAIRS, P, SEQ])
    inv_d = scratch("inv_d", [HEADS, SEQ])
    merged_d = scratch("merged_d", [NT, P, DC, 2, P])
    h_d = scratch("h_d", [SEQ, D])
    hn_d = scratch("hn_d", [SEQ, D])
    table_d = scratch("table_d", [SEQ * EXPERTS, 1], I32)
    jobs_d = scratch("jobs_d", [1, 1 + 2 * MORE_JOBS], I32)
    weight_d = scratch("weight_d", [P, 2 * NT])
    y_d = scratch("y_d", [2 * SEQ, D])

    with nc.cleanup_on_exit():
        stage_project(nc, x[0], meta, norm1_g[0], w_in[0], b_in[0], dw_w[0], dw_b[0], q_norm_g[0], k_norm_g[0],
                      b_forget[0], conv_d, gate_d, qk_d, v_d, decay_d)
    stage_attend(nc, qk_d, v_d, decay_d, o_d, inv_d)
    stage_merge(nc, conv_ln_g[0], conv_ln_b[0], w_conv_out[0], b_conv_out[0], w_attn_out[0], conv_d, gate_d,
                o_d, inv_d, merged_d)
    with ExitStack() as ctx:
        weights = ExpertWeights(ctx, nc, w_gate[0], w_up[0], w_down[0])
        stage_route(nc, x[0], norm2_g[0], w_out[0], w_group[0], b_group[0], w_router[0], b_router[0], merged_d,
                    h_d, hn_d, table_d, jobs_d, weight_d, weights)
        stage_experts(nc, weights, hn_d, table_d, jobs_d, y_d)
    stage_combine(nc, h_d, y_d, weight_d, out[0])


_INS = ["x", "meta", "norm1_g", "w_in", "b_in", "dw_w", "dw_b", "conv_ln_g", "conv_ln_b", "w_conv_out",
        "b_conv_out", "q_norm_g", "k_norm_g", "b_forget", "w_attn_out", "w_out", "norm2_g", "w_group",
        "b_group", "w_router", "b_router", "w_gate", "w_up", "w_down"]
_OUTS = [((1, SEQ, D), "float32")]


def kernel(**inputs):
    import numpy as _np
    import concourse.bacc as _bacc
    from concourse import mybir as _mybir
    from concourse.bass_utils import run_bass_kernel_spmd as _run

    nc = _bacc.Bacc("TRN2", target_bir_lowering=False, num_devices=1)
    arrays, args = {}, []
    for name in _INS:
        a = _np.ascontiguousarray(inputs[name])
        arrays[f"in_{name}_dram"] = a
        args.append(nc.dram_tensor(f"in_{name}_dram", a.shape, _mybir.dt.from_np(a.dtype), kind="ExternalInput").ap())
    for i, (shape, dtype) in enumerate(_OUTS):
        dt = _mybir.dt.from_np(_np.dtype(dtype))
        args.append(nc.dram_tensor(f"out_{i}_dram", shape, dt, kind="ExternalOutput").ap())
    hybrid_block(nc, *args)
    r = _run(nc, [arrays], core_ids=[0])
    got = tuple(r.results[0][f"out_{i}_dram"] for i in range(len(_OUTS)))
    return got[0]
```
